# Optimizing a Trainium2 kernel written in Bass

```python
import math
import jax, jax.numpy as jnp
from jax import lax
import numpy as np

D_MODEL = 1024
BATCH = 1
SEQ = 512
DEPTH = 2

HEAD_DIM = 64
NSA_HEADS = 8
NSA_KV_GROUPS = 2
NSA_WIDTH = NSA_HEADS * HEAD_DIM
ROPE_DIM = HEAD_DIM // 4
ROPE_THETA = 500000.0
CMP_LEN = 32
CMP_STRIDE = 16
CMP_HIDDEN = 128
SLC_LEN = 64
SLC_TOP = 16
WINDOW = 512
Q_BLOCK = 64
FORCE_SCORE = 1.0e4
NEG_INF = -1.0e30
SGU_WIDTH = 256
SGU_GROUPS = 4
SGU_CHUNK = 128
S5_WIDTH = 256
S5_GROUP_CH = 16
S5_GROUPS = S5_WIDTH // S5_GROUP_CH
S5_STATE = 64
MOE_GROUPS = 4
MOE_EXPERTS_PER_GROUP = 8
MOE_EXPERTS = MOE_GROUPS * MOE_EXPERTS_PER_GROUP
MOE_TOPK = 2
EXPERT_HIDDEN = 512
MOE_BLOCK = 128

RMS_EPS = 1e-6
KV_WIDTH = NSA_KV_GROUPS * HEAD_DIM
IN_PROJ_WIDTH = NSA_WIDTH + 6 * KV_WIDTH + 3 * NSA_HEADS + 2 * SGU_WIDTH + S5_WIDTH + 3 * D_MODEL

kernel_name = "hybrid_nsa_sgu_s5_hiermoe"

def _in_proj_split_points():
    sizes = (NSA_WIDTH, KV_WIDTH, KV_WIDTH, KV_WIDTH, KV_WIDTH, KV_WIDTH, KV_WIDTH,
             3 * NSA_HEADS, 2 * SGU_WIDTH, S5_WIDTH, 3 * D_MODEL)
    return [int(v) for v in np.cumsum(sizes)[:-1]]

def rms_norm(x, g):
    xf = x.astype(jnp.float32)
    y = xf * lax.rsqrt(jnp.mean(xf * xf, axis=-1, keepdims=True) + RMS_EPS)
    return (y * g.astype(jnp.float32)).astype(x.dtype)

def partial_rope(x, positions):
    half = ROPE_DIM // 2
    inv_freq = ROPE_THETA ** (-jnp.arange(half, dtype=jnp.float32) / half)
    ang = positions.astype(jnp.float32)[..., None] * inv_freq
    shp = ang.shape[:2] + (1,) * (x.ndim - 3) + (half,)
    cos, sin = jnp.cos(ang).reshape(shp), jnp.sin(ang).reshape(shp)
    xr = x[..., :ROPE_DIM].astype(jnp.float32)
    x1, x2 = xr[..., :half], xr[..., half:]
    rot = jnp.concatenate([x1 * cos - x2 * sin, x2 * cos + x1 * sin], axis=-1).astype(x.dtype)
    return jnp.concatenate([rot, x[..., ROPE_DIM:]], axis=-1)

def masked_softmax(scores, mask):
    s = jnp.where(mask, scores.astype(jnp.float32), NEG_INF)
    m = jnp.max(s, axis=-1, keepdims=True)
    e = jnp.where(mask, jnp.exp(s - m), 0.0)
    return e / jnp.maximum(jnp.sum(e, axis=-1, keepdims=True), 1e-30)

def compress_kv(kv, pos_emb, w1, w2):
    B, S, G, dh = kv.shape
    n_cmp = (S - CMP_LEN) // CMP_STRIDE + 1
    idx = np.arange(n_cmp)[:, None] * CMP_STRIDE + np.arange(CMP_LEN)[None, :]
    blocks = kv[:, idx] + pos_emb[None, None, :, None, :]
    flat = blocks.transpose(0, 1, 3, 2, 4).reshape(B, n_cmp, G, CMP_LEN * dh)
    return jax.nn.gelu(flat @ w1) @ w2

def _cmp_to_slc_overlap(n_cmp, n_slc):
    c0 = np.arange(n_cmp)[:, None] * CMP_STRIDE
    s0 = np.arange(n_slc)[None, :] * SLC_LEN
    ov = np.clip(np.minimum(c0 + CMP_LEN, s0 + SLC_LEN) - np.maximum(c0, s0), 0, None)
    return (ov / CMP_LEN).astype(np.float32)

def nsa_attention(q, k_cmp, v_cmp, k_slc, v_slc, k_win, v_win, gates, positions,
                  cmp_pos_k, cmp_pos_v, cmp_k_w1, cmp_k_w2, cmp_v_w1, cmp_v_w2):
    B, S, G, R, dh = q.shape
    scale = dh ** -0.5
    q_rot = partial_rope(q, positions)
    k_slc = partial_rope(k_slc, positions)
    k_win = partial_rope(k_win, positions)
    kc = compress_kv(k_cmp, cmp_pos_k, cmp_k_w1, cmp_k_w2)
    vc = compress_kv(v_cmp, cmp_pos_v, cmp_v_w1, cmp_v_w2)
    n_cmp = kc.shape[1]
    n_slc = S // SLC_LEN
    n_top = min(SLC_TOP, n_slc)
    cmp_end = jnp.asarray(np.arange(n_cmp) * CMP_STRIDE + CMP_LEN - 1, dtype=jnp.int32)
    overlap = jnp.asarray(_cmp_to_slc_overlap(n_cmp, n_slc))
    k_blocks = k_slc.reshape(B, n_slc, SLC_LEN, G, dh).transpose(0, 3, 1, 2, 4)
    v_blocks = v_slc.reshape(B, n_slc, SLC_LEN, G, dh).transpose(0, 3, 1, 2, 4)
    k_win_p = jnp.concatenate([jnp.zeros((B, WINDOW, G, dh), k_win.dtype), k_win], axis=1)
    v_win_p = jnp.concatenate([jnp.zeros((B, WINDOW, G, dh), v_win.dtype), v_win], axis=1)
    b_idx = jnp.arange(B)[:, None, None, None]
    g_idx = jnp.arange(G)[None, None, :, None]
    slc_ids = jnp.arange(n_slc)

    def query_block(i):
        t0 = i * Q_BLOCK
        t = t0 + jnp.arange(Q_BLOCK)
        qb = lax.dynamic_slice_in_dim(q, t0, Q_BLOCK, 1)
        qrb = lax.dynamic_slice_in_dim(q_rot, t0, Q_BLOCK, 1)
        gb = lax.dynamic_slice_in_dim(gates, t0, Q_BLOCK, 1)
        s_c = jnp.einsum('bqgrd,bcgd->bqgrc', qb, kc) * scale
        m_c = (cmp_end[None, :] <= t[:, None])[None, :, None, None, :]
        p_c = masked_softmax(s_c, m_c)
        o_c = jnp.einsum('bqgrc,bcgd->bqgrd', p_c.astype(vc.dtype), vc)
        imp = jnp.einsum('bqgrc,cj->bqgj', p_c, overlap)
        blk_t = (t // SLC_LEN)[:, None]
        causal = slc_ids[None, :] <= blk_t
        forced = (slc_ids[None, :] == 0) | (slc_ids[None, :] == blk_t) | (slc_ids[None, :] == blk_t - 1)
        imp = jnp.where(forced[None, :, None, :], FORCE_SCORE, imp)
        imp = jnp.where(causal[None, :, None, :], imp, NEG_INF)
        top_v, top_i = lax.top_k(imp, n_top)
        kg = k_blocks[b_idx, g_idx, top_i]
        vg = v_blocks[b_idx, g_idx, top_i]
        key_pos = top_i[..., None] * SLC_LEN + jnp.arange(SLC_LEN)
        m_s = (top_v > 0.5 * NEG_INF)[..., None] & (key_pos <= t[None, :, None, None, None])
        s_s = jnp.einsum('bqgrd,bqgnld->bqgrnl', qrb, kg) * scale
        p_s = masked_softmax(s_s.reshape(B, Q_BLOCK, G, R, n_top * SLC_LEN),
                             m_s.reshape(B, Q_BLOCK, G, 1, n_top * SLC_LEN))
        o_s = jnp.einsum('bqgrnl,bqgnld->bqgrd',
                         p_s.reshape(B, Q_BLOCK, G, R, n_top, SLC_LEN).astype(vg.dtype), vg)
        kw = lax.dynamic_slice_in_dim(k_win_p, t0, WINDOW + Q_BLOCK, 1)
        vw = lax.dynamic_slice_in_dim(v_win_p, t0, WINDOW + Q_BLOCK, 1)
        s_pos = t0 - WINDOW + jnp.arange(WINDOW + Q_BLOCK)
        diff = t[:, None] - s_pos[None, :]
        m_w = ((s_pos[None, :] >= 0) & (diff >= 0) & (diff < WINDOW))[None, :, None, None, :]
        s_w = jnp.einsum('bqgrd,bkgd->bqgrk', qrb, kw) * scale
        p_w = masked_softmax(s_w, m_w)
        o_w = jnp.einsum('bqgrk,bkgd->bqgrd', p_w.astype(vw.dtype), vw)
        return gb[..., 0:1] * o_c + gb[..., 1:2] * o_s + gb[..., 2:3] * o_w

    out = lax.map(query_block, jnp.arange(S // Q_BLOCK))
    return jnp.moveaxis(out, 0, 1).reshape(B, S, G * R * dh)

def spatial_gating(uv, norm_g, w_s, b_s):
    z = jax.nn.gelu(uv)
    u, v = jnp.split(z, 2, axis=-1)
    v = rms_norm(v, norm_g)
    B, S, _ = v.shape
    vg = v.reshape(B, S // SGU_CHUNK, SGU_CHUNK, SGU_GROUPS, SGU_WIDTH // SGU_GROUPS)
    tril = jnp.asarray(np.tril(np.ones((SGU_CHUNK, SGU_CHUNK), dtype=bool)))
    w = jnp.where(tril[None], w_s, 0.0).astype(v.dtype)
    mixed = jnp.einsum('gts,bcsgd->bctgd', w, vg) + b_s.T[None, None, :, :, None].astype(v.dtype)
    return u * mixed.reshape(B, S, SGU_WIDTH)

def s5_layer(xs, a_re, a_im, log_step, b_re, b_im, c_re, c_im, d, glu_w, glu_b):
    B, S, _ = xs.shape
    f32 = jnp.float32
    xg = xs.reshape(B, S, S5_GROUPS, S5_GROUP_CH).astype(f32)
    a_re, a_im = a_re.astype(f32), a_im.astype(f32)
    step = jnp.exp(log_step.astype(f32))[:, None]
    mag = jnp.exp(a_re * step)
    abar_re, abar_im = mag * jnp.cos(a_im * step), mag * jnp.sin(a_im * step)
    den = a_re * a_re + a_im * a_im
    nr, ni = abar_re - 1.0, abar_im
    coef_re = (nr * a_re + ni * a_im) / den
    coef_im = (ni * a_re - nr * a_im) / den
    b_re, b_im = b_re.astype(f32), b_im.astype(f32)
    bbar_re = coef_re[..., None] * b_re - coef_im[..., None] * b_im
    bbar_im = coef_re[..., None] * b_im + coef_im[..., None] * b_re
    bu_re = jnp.einsum('bsgh,gph->bsgp', xg, bbar_re)
    bu_im = jnp.einsum('bsgh,gph->bsgp', xg, bbar_im)
    ar = jnp.broadcast_to(abar_re, bu_re.shape)
    ai = jnp.broadcast_to(abar_im, bu_re.shape)

    def combine(e1, e2):
        a1r, a1i, b1r, b1i = e1
        a2r, a2i, b2r, b2i = e2
        return (a2r * a1r - a2i * a1i, a2r * a1i + a2i * a1r,
                a2r * b1r - a2i * b1i + b2r, a2r * b1i + a2i * b1r + b2i)

    _, _, h_re, h_im = lax.associative_scan(combine, (ar, ai, bu_re, bu_im), axis=1)
    y = (jnp.einsum('bsgp,ghp->bsgh', h_re, c_re.astype(f32))
         - jnp.einsum('bsgp,ghp->bsgh', h_im, c_im.astype(f32)))
    y = y + d.astype(f32).reshape(S5_GROUPS, S5_GROUP_CH) * xg
    y = jax.nn.gelu(y.reshape(B, S, S5_WIDTH))
    y = y * jax.nn.sigmoid(y @ glu_w.astype(f32) + glu_b.astype(f32))
    return y.astype(xs.dtype)

def routed_experts(xf, expert, weight, w_gate, w_up, w_down):
    T, D = xf.shape
    TK = expert.shape[0]
    n_exp = w_gate.shape[0]
    order = jnp.argsort(expert)
    e_sorted = expert[order]
    tok_sorted = order // MOE_TOPK
    counts = jnp.bincount(expert, length=n_exp)
    padded = (counts + MOE_BLOCK - 1) // MOE_BLOCK * MOE_BLOCK
    start = jnp.cumsum(counts) - counts
    end_p = jnp.cumsum(padded)
    start_p = end_p - padded
    dest = start_p[e_sorted] + jnp.arange(TK) - start[e_sorted]
    n_rows = TK + n_exp * MOE_BLOCK
    n_blocks = n_rows // MOE_BLOCK
    x_buf = jnp.zeros((n_rows, D), xf.dtype).at[dest].set(xf[tok_sorted])
    blk_exp = jnp.minimum(jnp.searchsorted(end_p, jnp.arange(n_blocks) * MOE_BLOCK, side='right'), n_exp - 1)

    def expert_block(args):
        xb, e = args
        hid = jax.nn.silu(xb @ w_gate[e]) * (xb @ w_up[e])
        return hid @ w_down[e]

    y_buf = lax.map(expert_block, (x_buf.reshape(n_blocks, MOE_BLOCK, D), blk_exp)).reshape(n_rows, D)
    y = y_buf[dest] * weight[order][:, None].astype(y_buf.dtype)
    return jax.ops.segment_sum(y, tok_sorted, num_segments=T)

def hierarchical_moe(h, router_group_w, router_group_b, router_expert_w, router_expert_b,
                     expert_w_gate, expert_w_up, expert_w_down):
    B, S, D = h.shape
    T = B * S
    xf = h.reshape(T, D)
    grp_logits = (xf @ router_group_w).astype(jnp.float32) + router_group_b.astype(jnp.float32)
    grp_prob = jax.nn.softmax(grp_logits, axis=-1)
    grp = jnp.argmax(grp_logits, axis=-1).astype(jnp.int32)
    grp_w = jnp.take_along_axis(grp_prob, grp[:, None], axis=-1)
    exp_logits = ((xf @ router_expert_w).astype(jnp.float32) + router_expert_b.astype(jnp.float32)
                  ).reshape(T, MOE_GROUPS, MOE_EXPERTS_PER_GROUP)
    exp_logits = jnp.take_along_axis(exp_logits, grp[:, None, None], axis=1)[:, 0]
    exp_prob = jax.nn.softmax(exp_logits, axis=-1)
    top_p, top_j = lax.top_k(exp_prob, MOE_TOPK)
    combine = grp_w * top_p / jnp.sum(top_p, axis=-1, keepdims=True)
    expert = grp[:, None] * MOE_EXPERTS_PER_GROUP + top_j.astype(jnp.int32)
    y = routed_experts(xf, expert.reshape(-1), combine.reshape(-1), expert_w_gate, expert_w_up, expert_w_down)
    return y.reshape(B, S, D)

def setup_inputs(seed: int = 0) -> dict:
    key = jax.random.key(seed)
    ks = iter(jax.random.split(key, 48))
    L = DEPTH

    def nrm(shape, scale):
        return jax.random.normal(next(ks), shape, jnp.float32) * scale

    x = nrm((BATCH, SEQ, D_MODEL), 1.0)
    offset = jax.random.randint(next(ks), (BATCH, 1), 0, 1024, dtype=jnp.int32)
    positions = offset + jnp.arange(SEQ, dtype=jnp.int32)[None, :]
    return {
        "x": x,
        "positions": positions,
        "norm_mix_g": 1.0 + nrm((L, D_MODEL), 0.02),
        "w_in": nrm((L, D_MODEL, IN_PROJ_WIDTH), D_MODEL ** -0.5),
        "cmp_pos_k": nrm((L, CMP_LEN, HEAD_DIM), 0.02),
        "cmp_pos_v": nrm((L, CMP_LEN, HEAD_DIM), 0.02),
        "cmp_k_w1": nrm((L, CMP_LEN * HEAD_DIM, CMP_HIDDEN), (CMP_LEN * HEAD_DIM) ** -0.5),
        "cmp_k_w2": nrm((L, CMP_HIDDEN, HEAD_DIM), CMP_HIDDEN ** -0.5),
        "cmp_v_w1": nrm((L, CMP_LEN * HEAD_DIM, CMP_HIDDEN), (CMP_LEN * HEAD_DIM) ** -0.5),
        "cmp_v_w2": nrm((L, CMP_HIDDEN, HEAD_DIM), CMP_HIDDEN ** -0.5),
        "w_attn_o": nrm((L, NSA_WIDTH, D_MODEL), NSA_WIDTH ** -0.5),
        "sgu_norm_g": 1.0 + nrm((L, SGU_WIDTH), 0.02),
        "sgu_w": nrm((L, SGU_GROUPS, SGU_CHUNK, SGU_CHUNK), 0.5 * SGU_CHUNK ** -0.5),
        "sgu_b": 1.0 + nrm((L, SGU_GROUPS, SGU_CHUNK), 0.02),
        "w_sgu_o": nrm((L, SGU_WIDTH, D_MODEL), SGU_WIDTH ** -0.5),
        "s5_a_re": -0.5 + nrm((L, S5_GROUPS, S5_STATE), 0.01),
        "s5_a_im": math.pi * jnp.arange(S5_STATE, dtype=jnp.float32) + nrm((L, S5_GROUPS, S5_STATE), 0.01),
        "s5_log_step": jax.random.uniform(next(ks), (L, S5_GROUPS), jnp.float32, math.log(1e-3), math.log(1e-1)),
        "s5_b_re": nrm((L, S5_GROUPS, S5_STATE, S5_GROUP_CH), (2 * S5_GROUP_CH) ** -0.5),
        "s5_b_im": nrm((L, S5_GROUPS, S5_STATE, S5_GROUP_CH), (2 * S5_GROUP_CH) ** -0.5),
        "s5_c_re": nrm((L, S5_GROUPS, S5_GROUP_CH, S5_STATE), (2 * S5_STATE) ** -0.5),
        "s5_c_im": nrm((L, S5_GROUPS, S5_GROUP_CH, S5_STATE), (2 * S5_STATE) ** -0.5),
        "s5_d": nrm((L, S5_WIDTH), 0.5),
        "s5_glu_w": nrm((L, S5_WIDTH, S5_WIDTH), S5_WIDTH ** -0.5),
        "s5_glu_b": nrm((L, S5_WIDTH), 0.01),
        "w_s5_o": nrm((L, S5_WIDTH, D_MODEL), S5_WIDTH ** -0.5),
        "w_mix_o": nrm((L, D_MODEL, D_MODEL), D_MODEL ** -0.5),
        "norm_ffn_g": 1.0 + nrm((L, D_MODEL), 0.02),
        "router_group_w": nrm((L, D_MODEL, MOE_GROUPS), D_MODEL ** -0.5),
        "router_group_b": nrm((L, MOE_GROUPS), 0.01),
        "router_expert_w": nrm((L, D_MODEL, MOE_EXPERTS), D_MODEL ** -0.5),
        "router_expert_b": nrm((L, MOE_EXPERTS), 0.01),
        "expert_w_gate": nrm((L, MOE_EXPERTS, D_MODEL, EXPERT_HIDDEN), D_MODEL ** -0.5),
        "expert_w_up": nrm((L, MOE_EXPERTS, D_MODEL, EXPERT_HIDDEN), D_MODEL ** -0.5),
        "expert_w_down": nrm((L, MOE_EXPERTS, EXPERT_HIDDEN, D_MODEL), EXPERT_HIDDEN ** -0.5),
        "norm_final_g": 1.0 + nrm((D_MODEL,), 0.02),
    }

def reference(x, positions, norm_mix_g, w_in, cmp_pos_k, cmp_pos_v, cmp_k_w1, cmp_k_w2,
              cmp_v_w1, cmp_v_w2, w_attn_o, sgu_norm_g, sgu_w, sgu_b, w_sgu_o,
              s5_a_re, s5_a_im, s5_log_step, s5_b_re, s5_b_im, s5_c_re, s5_c_im, s5_d,
              s5_glu_w, s5_glu_b, w_s5_o, w_mix_o, norm_ffn_g, router_group_w, router_group_b,
              router_expert_w, router_expert_b, expert_w_gate, expert_w_up, expert_w_down,
              norm_final_g):
    B, S, D = x.shape
    G, R = NSA_KV_GROUPS, NSA_HEADS // NSA_KV_GROUPS
    split_points = _in_proj_split_points()
    for l in range(DEPTH):
        h = rms_norm(x, norm_mix_g[l])
        parts = jnp.split(h @ w_in[l], split_points, axis=-1)
        q, k_c, v_c, k_s, v_s, k_w, v_w, nsa_g, sgu_in, s5_in, branch_g = parts
        q = q.reshape(B, S, G, R, HEAD_DIM)
        kv = [t.reshape(B, S, G, HEAD_DIM) for t in (k_c, v_c, k_s, v_s, k_w, v_w)]
        nsa_gates = jax.nn.sigmoid(nsa_g.astype(jnp.float32)).astype(q.dtype).reshape(B, S, G, R, 3)
        y_a = nsa_attention(q, kv[0], kv[1], kv[2], kv[3], kv[4], kv[5], nsa_gates, positions,
                            cmp_pos_k[l], cmp_pos_v[l], cmp_k_w1[l], cmp_k_w2[l],
                            cmp_v_w1[l], cmp_v_w2[l]) @ w_attn_o[l]
        y_b = spatial_gating(sgu_in, sgu_norm_g[l], sgu_w[l], sgu_b[l]) @ w_sgu_o[l]
        y_c = s5_layer(s5_in, s5_a_re[l], s5_a_im[l], s5_log_step[l], s5_b_re[l], s5_b_im[l],
                       s5_c_re[l], s5_c_im[l], s5_d[l], s5_glu_w[l], s5_glu_b[l]) @ w_s5_o[l]
        g_a, g_b, g_c = jnp.split(jax.nn.sigmoid(branch_g.astype(jnp.float32)), 3, axis=-1)
        merged = (g_a * y_a + g_b * y_b + g_c * y_c).astype(h.dtype)
        x = x + merged @ w_mix_o[l]
        h = rms_norm(x, norm_ffn_g[l])
        x = x + hierarchical_moe(h, router_group_w[l], router_group_b[l], router_expert_w[l],
                                 router_expert_b[l], expert_w_gate[l], expert_w_up[l], expert_w_down[l])
    return rms_norm(x, norm_final_g)


_drawn_inputs = setup_inputs


def setup_inputs(seed=0):
    import zlib

    import numpy as np

    out = dict(_drawn_inputs(seed))
    spreads = {}
    factors = {'cmp_pos_k': 24.472,
     'cmp_pos_v': 3.393,
     'sgu_norm_g': 3.498,
     's5_a_re': 200.0,
     's5_b_im': 9.452,
     's5_glu_b': 25.431,
     'router_group_b': 2.697,
     'router_expert_b': 3.141,
     'norm_final_g': 25.457,
     's5_b_re': 4.817,
     's5_c_re': 2.833,
     's5_c_im': 3.806}
    for name, (base, spread) in spreads.items():
        noise = np.random.default_rng([zlib.crc32(name.encode()), seed]).standard_normal(out[name].shape)
        drawn = base * np.exp(spread * noise) if base else spread * noise
        out[name] = __import__('jax').numpy.asarray(drawn.astype(out[name].dtype))
    for name, factor in factors.items():
        out[name] = (out[name] * factor).astype(out[name].dtype)
    return out
```

```python
from contextlib import ExitStack

import numpy as np

import concourse.bass as bass
from concourse import mybir

F32 = mybir.dt.float32
I32 = mybir.dt.int32
ALU = mybir.AluOpType
ACT = mybir.ActivationFunctionType
AX = mybir.AxisListType.X

P = 128
D = 1024
S = 512
L = 2
NT = S // P
ND = D // P
H, G, R, DH = 8, 2, 4, 64
NCMP = 31
HALF_ROPE = 8
N_EXP, N_GRP, E_PER = 32, 4, 8
HID = 512
NH = HID // P
CAP = 64
SG = 4
NCH = 8
EPS = 1e-6
NEG = -1.0e30
MAGIC = 12582912.0
TWO_PI = 2.0 * np.pi
PI_1 = 6.28125
PI_2 = float(np.float32(np.round((TWO_PI - PI_1) * 2.0**19) / 2.0**19))
PI_3 = float(np.float32(TWO_PI - PI_1 - PI_2))
PI_SAFE = 3.1415925

SMALL = dict(gmix=(0, 8), gffn=(8, 8), a_re=(16, 8), a_im=(24, 8), lstep=(32, 8), d=(40, 2), glub=(42, 2),
             sgub=(44, 4), w2v=(48, 64), w2k=(112, 128), posk=(240, 32), posv=(272, 32), wnsa=(304, 192))
N_SMALL = 496
C_IDENT, C_ROT, C_CAUSAL, C_CADD, C_C01, C_FREQ = 0, 128, 256, 384, 512, 640
N_CONST = 641
M_TRI, M_ONES, M_IOTA, M_DESC32, M_BASE, M_DESC4 = 0, 128, 256, 320, 352, 384
N_MCONST = 388

O_X = 0
O_XN = 4096
O_HT = 8192
O_SLAB = 12288
O_GATE = 24576
O_KS = 36864
O_KW = 37888
O_KC = 38912
O_V = 41984
O_Z = 43104
O_OACC = 45152
O_YST = 47200
O_XS = 48224
O_S5 = 49248
O_CONST = 50272
O_ROPE = O_CONST + N_CONST
O_SMALL = O_ROPE + 1024
O_BBT = O_SMALL + N_SMALL
O_STAT = O_BBT + 512
N_STAT = 192
O_END = O_STAT + N_STAT
assert O_END <= 53215

SLAB = 4096
J_HT, J_SGU, J_S5, J_KC, J_KS, J_Q, J_V, J_NSA, J_GATE, J_MIX, J_H2 = 0, 8, 12, 14, 16, 18, 22, 26, 27, 51, 59
J_END = 67
N_ATT = 2 * NT * H
CRED = 2


def build(nc, io):
    ctx = ExitStack()
    with ctx:
        def sem(name):
            return ctx.enter_context(nc.semaphore(name))

        arena = ctx.enter_context(nc.sbuf_tensor("arena", [P, O_END], F32))
        ps = ctx.enter_context(nc.psum_tensor("ps", [P, 8, 512], F32))

        def view(off, *dims):
            n = int(np.prod(dims))
            a = arena[:, off:off + n]
            if len(dims) == 1:
                return a
            names = "abcd"[:len(dims)]
            return a.rearrange("p (" + " ".join(names) + ") -> p " + " ".join(names),
                               **{k: v for k, v in zip(names[1:], dims[1:])})

        x = view(O_X, NT, D)
        xn = view(O_XN, NT, D)
        q_plain = view(O_XN, 4, S)
        q_rot = view(O_XN + 2048, 4, S)
        hT = view(O_HT, ND, S)
        slab = [O_SLAB + i * SLAB for i in range(3)]
        tab_re = view(O_GATE, NCH, S)
        tab_im = view(O_GATE + 4096, NCH, S)
        tab_tmp = O_GATE + 8192
        sgu_w = view(O_GATE + 10240, SG, P)
        sgu_g = view(O_GATE + 10752, 256)
        s5_c = view(O_GATE + 10240, S)
        s5_d = view(O_GATE + 10752, S)
        s5_ab = [[view(O_Z + (2 * b + i) * S, S) for i in range(2)] for b in range(2)]
        gates = view(O_GATE, 24, S)
        k_sel = view(O_KS, 2, S)
        k_win = view(O_KW, 2, S)
        c_in = [view(O_KC, 3, S), view(O_KC + 1536, 3, S)]
        oT = view(O_KC, 4, S)
        O_CW = O_KC + 2048
        v_cmp = view(O_CW, G, R * DH)
        k_cmp = view(O_CW + 512, G, 32)
        k_hid = view(O_CW + 576, G, 32)
        v_hid = view(O_CW + 640, G, R, 32)
        c_bias = view(O_CW + 896, 2)
        c_max = view(O_CW + 898, 32)
        c_sum = view(O_CW + 930, 32)
        o_tmp = view(O_CW, S)
        v_tok = view(O_V, NT, 256)
        nsa_g = view(O_V + 1024, NT, 24)
        z = view(O_Z, NT, S)
        prob = [view(O_Z + i * S, S) for i in range(2)]
        probT = [view(O_Z + 1024 + i * S, S) for i in range(2)]
        c_sc = view(O_Z, NT, H, 32)
        c_scf = view(O_Z, NT * H, 32)
        m_tmp = [view(O_Z + i * S, S) for i in range(2)]
        vn = view(O_OACC, NT, 256)
        ys = view(O_OACC + 1024, NT, 256)
        cc = view(O_OACC, 2, NCH, 32)
        glu_w = view(O_OACC + 512, 2, 256)
        oacc = view(O_OACC, NT, S)
        ysT = view(O_YST, 2, S)
        b_in = view(O_YST, 2, NCH, 32)
        s5_small = [view(O_YST + 512 + 8 * i, 8) for i in range(16)]
        xsT = view(O_XS, 2, S)
        s5T = view(O_S5, 2, S)
        bbar = view(O_S5, 2, NCH, 32)
        bb_tmp = view(O_S5 + 512, NCH, 32)
        cst = view(O_CONST, N_CONST)
        ident = cst[:, C_IDENT:C_IDENT + P]
        rot = cst[:, C_ROT:C_ROT + P]
        causal = cst[:, C_CAUSAL:C_CAUSAL + P]
        c_add = view(O_CONST + C_CADD, NT, 32)
        c_01 = view(O_CONST + C_C01, NT, 32)
        freq = cst[:, C_FREQ:C_FREQ + 1]
        rope_cos = view(O_ROPE, S)
        rope_sin = view(O_ROPE + S, S)
        small = {k: view(O_SMALL + a, n) for k, (a, n) in SMALL.items()}
        wnsa = view(O_SMALL + SMALL["wnsa"][0], ND, 24)
        bbT = view(O_BBT, 2, 2, P)
        st = O_STAT
        mag = view(st, 8)
        cos1 = view(st + 8, 8)
        sin1 = view(st + 16, 8)
        pw = [view(st + 24 + 8 * i, 8) for i in range(4)]
        sumsq = view(st + 56, 4)
        rstd = view(st + 60, 4)
        vsumsq = view(st + 64, 4)
        vrstd = view(st + 68, 4)
        rowmax = view(st + 72, 4)
        rowsum = view(st + 76, N_ATT)
        rinv = view(st + 140, 8)
        wgt = view(st + 148, 8)
        glub_h = view(st + 156, 2)
        sincos = [view(st + 160 + 8 * i, 8) for i in range(4)]

        A = O_KS
        mc = view(A, N_MCONST)
        tri = mc[:, M_TRI:M_TRI + P]
        ones = mc[:, M_ONES:M_ONES + P]
        iota = mc[:, M_IOTA:M_IOTA + CAP]
        desc32 = mc[:, M_DESC32:M_DESC32 + 32]
        base_e = mc[:, M_BASE:M_BASE + 32]
        desc4 = mc[:, M_DESC4:M_DESC4 + 4]
        A += N_MCONST
        rw = view(A, ND, 36)
        rb = view(A + 288, 36)
        A += 324
        logit = view(A, NT, 36); A += 144
        gtmp = view(A, NT, 4); A += 16
        goh = view(A, NT, 4); A += 16
        em = view(A, NT, 32); A += 128
        eq = view(A, NT, 32); A += 128
        oh = [view(A + 128 * i, NT, 32) for i in range(2)]; A += 256
        sel_all = view(A, NT, 32); A += 128
        rank = view(A, NT, 32); A += 128
        slot = view(A, 33, NT); A += 132
        r1 = [view(A + 4 * i, NT) for i in range(10)]; A += 40
        cw = [view(A + 4 * i, NT) for i in range(2)]; A += 8
        cwm = [view(A + 4 * i, NT) for i in range(2)]; A += 8
        didx = [view(A + 4 * i, NT).bitcast(I32) for i in range(2)]; A += 8
        countf = view(A, N_EXP + 1); A += 34
        counts = view(A, N_EXP + 1).bitcast(I32); A += 34
        selm = [view(A + 256 * i, NT, CAP) for i in range(2)]; A += 512
        xeT = [view(A + 512 * i, ND, CAP) for i in range(2)]; A += 1024
        silu = view(A, HID); A += 512
        hid = view(A, HID); A += 512
        hidT = [view(A + 256 * i, NH, CAP) for i in range(2)]; A += 512
        ybuf = [view(A + 512 * i, 512) for i in range(2)]; A += 1024
        assert A <= O_CONST
        wslot = [[O_GATE + i * SLAB for i in range(3)], [O_SLAB + i * SLAB for i in range(3)]]
        w_gate = [view(w[0], ND, HID) for w in wslot]
        w_up = [view(w[1], ND, HID) for w in wslot]
        w_down = [view(w[2], NH, D) for w in wslot]
        yg = [[view(O_SLAB + (4 * k + t) * D, D) for t in range(NT)] for k in range(2)]

        gf = small["gffn"].unsqueeze(2).to_broadcast([P, ND, CAP])

        def build_sel(e, buf):
            return nc.vector.tensor_tensor(selm[buf], iota.unsqueeze(1).to_broadcast([P, NT, CAP]),
                                   slot[:, bass.ds(e, 1), :].rearrange("p e t -> p (e t)").unsqueeze(2)
                                   .to_broadcast([P, NT, CAP]), ALU.is_equal)

        def take_x(b, bank):
            return nc.vector.tensor_tensor(xeT[b], ps[:, bank, :].rearrange("p (a b) -> p a b", a=ND), gf, ALU.mult)

        BANK_P, BANK_S, BANK_T, BANK_O = [0, 1], [2, 3], [4, 5], [6, 7]

        s = {n: sem(n) for n in ("pro_in", "pro_dve", "pro_act")}
        pos_i = view(O_XN, S).bitcast(I32)
        ang, kk, rr, r2 = (view(O_XN + 512 * i, S) for i in range(1, 5))
        with nc.Block() as block:
            @block.sync
            def _(sp):
                sp.dma_start(x, io["x"].rearrange("b (t p) d -> p (b t) d", p=P)).then_inc(s["pro_in"], 16)
                sp.dma_start(cst, io["consts"]).then_inc(s["pro_in"], 16)
                sp.dma_start(pos_i, io["positions"].to_broadcast([P, S])).then_inc(s["pro_in"], 16)

            @block.vector
            def _(dve):
                dve.wait_ge(s["pro_in"], 48)
                n = 0

                def link(ins):
                    nonlocal n
                    ins.then_inc(s["pro_dve"], 1)
                    n += 1
                    dve.wait_ge(s["pro_dve"], n)
                link(nc.vector.tensor_copy(rr, pos_i))
                link(nc.vector.tensor_scalar(ang, rr, freq, None, ALU.mult))
                reduce_angle(nc, link, ang, kk, rr, r2)

            @block.scalar
            def _(act):
                act.wait_ge(s["pro_dve"], 2 + N_REDUCE)
                nc.scalar.activation(rope_sin, rr, ACT.Sin).then_inc(s["pro_act"], 1)
                nc.scalar.activation(rope_cos, r2, ACT.Sin).then_inc(s["pro_act"], 1)
                act.wait_ge(s["pro_act"], 2)

        names = ("small_in", "bparam_in", "sgu_in", "cglu_in", "router_in", "mconst_in", "slab_in0", "slab_in1", "slab_in2",
                 "chain_dve", "chain_act", "chain_pool", "sumsq_ready", "var_ready", "sd_ready", "xn_ready",
                 "step_ready", "lam_ready", "mag_ready", "angle_ready", "sincos_ready", "table_ready",
                 "planes_clear", "bb_ready", "bb_done", "bb_evac", "proj_done", "proj_free",
                 "vsq_ready", "vvar_ready", "vsd_ready", "vn_ready", "sgu_w_ready", "mixed_done", "mixed_evac", "ysT_done", "ysT_evac",
                 "bu_done", "twist_read", "h_ready", "y_done", "rot_done", "rope_done", "y1_ready", "gelu_done",
                 "glu_done", "glu_read", "s5_done", "hidden_done", "hid_ready", "ckv_done", "ckv_ready", "cs_done", "cs_read",
                 "cexp_in", "cexp_done", "cp_ready", "ct_done", "ct_evac", "oc_done", "oc_evac",
                 "scores_done", "max_done", "exp_done", "tr_done", "pt_evac", "pv_done", "o_evac",
                 "oT_done", "oT_evac", "outp_done", "merge_done", "nsa_tanh", "nsa_ready",
                 "rt_done", "gexp_in", "gexp_done", "e2_in", "e2_done", "sel_ready", "rank_done", "route_done",
                 "x_gathered", "sel_built", "xe_ready", "gu_done", "silu_done", "hid_done", "hT_done", "hT_read",
                 "down_done", "y_read", "y_out0", "y_out1",
                 "we0g", "we0u", "we0d", "we1g", "we1u", "we1d", "yg_in", "comb_done")
        s.update({n: sem(n) for n in names})
        slab_in = [s["slab_in0"], s["slab_in1"], s["slab_in2"]]
        y_out = [s["y_out0"], s["y_out1"]]
        w_in_sem = [[s["we0g"], s["we0u"], s["we0d"]], [s["we1g"], s["we1u"], s["we1d"]]]
        over_names = ("ov_shift", "ov_weights", "ov_sel", "ov_gathered", "ov_xe", "ov_gu", "ov_wt", "ov_selw", "ov_selT",
                      "ov_silu", "ov_hid", "ov_hT", "ov_hT_read", "ov_selT_read", "ov_down", "ov_y", "ov_back", "ov_added")
        so = {n: sem(n) for n in over_names}
        over_sems = list(so.values())
        layer_sems = [s[n] for n in names if n != "yg_in"]

        with nc.Fori(0, L) as layer:
            def row(ap):
                return ap[bass.ds(layer, 1)].rearrange("l p n -> (l p) n")

            def expert_rows(ap, e, k):
                return ap[bass.ds(layer, 1), bass.ds(e, 1)].rearrange("l e (k p) n -> p (l e k) n", p=P, k=k)

            with nc.Block() as block:
                @block.sync
                def _(sp):
                    sp.dma_start(view(O_SMALL, N_SMALL), row(io["small"])).then_inc(s["small_in"], 16)
                    sp.dma_start(view(O_YST, 512), row(io["bparam"])).then_inc(s["bparam_in"], 16)
                    sp.dma_start(view(O_GATE + 10240, 768), row(io["sgup"])).then_inc(s["sgu_in"], 16)
                    free = {3: (s["proj_done"], J_S5), 4: (s["proj_done"], J_KS), 5: (s["proj_done"], J_KS + 4),
                            6: (s["proj_done"], J_NSA), 7: (s["hidden_done"], 1), 8: (s["hidden_done"], 2),
                            15: (s["outp_done"], ND)}
                    for k in range(9, 15):
                        free[k] = (s["proj_done"], J_GATE + 4 * (k - 9) + 4)
                    for k in range(16):
                        if k in free:
                            sp.wait_ge(*free[k])
                        if k == 4:
                            sp.wait_ge(s["ysT_done"], 2)
                            sp.dma_start(view(O_OACC, 1024), row(io["cglu"])).then_inc(s["cglu_in"], 16)
                        src = io["dense"][bass.ds(layer, 1), k].rearrange("l p n -> (l p) n")
                        sp.dma_start(view(slab[k % 3], SLAB), src).then_inc(slab_in[k % 3], 16)
                    sp.wait_ge(s["merge_done"], ND)
                    load_expert(nc, sp, io, expert_rows, 0, 0, w_gate, w_up, w_down, w_in_sem)
                    sp.wait_ge(s["outp_done"], ND)
                    sp.dma_start(view(O_KS + N_MCONST, 324), row(io["router"])).then_inc(s["router_in"], 16)
                    sp.dma_start(mc, io["mconsts"]).then_inc(s["mconst_in"], 16)
                    sp.wait_ge(s["proj_done"], J_H2)
                    load_expert(nc, sp, io, expert_rows, 1, 1, w_gate, w_up, w_down, w_in_sem)
                    with sp.Fori(0, N_EXP // 2 - 1) as i:
                        for b in range(2):
                            e = 2 * i + 2 + b
                            sp.wait_ge(s["gu_done"], 2 * i + b + 1 + CRED)
                            sp.dma_start(w_gate[b], expert_rows(io["expert_w_gate"], e, ND)).then_inc(w_in_sem[b][0], 16)
                            sp.dma_start(w_up[b], expert_rows(io["expert_w_up"], e, ND)).then_inc(w_in_sem[b][1], 16)
                            sp.wait_ge(s["down_done"], 2 * i + b + 1 + CRED)
                            sp.dma_start(w_down[b], expert_rows(io["expert_w_down"], e, NH)).then_inc(w_in_sem[b][2], 16)

                @block.tensor
                def _(pe):
                    def wait_slab(k):
                        pe.wait_ge(slab_in[k % 3], 16 * (k // 3 + 1))

                    def bank_p(n):
                        if n >= 2:
                            pe.wait_ge(s["proj_free"], n - 1)
                        return ps[:, BANK_P[n % 2], :]

                    def feature_job(n, w, col):
                        out = bank_p(n)
                        for k in range(ND):
                            last = nc.tensor.matmul(out, w[:, k, col:col + P], hT[:, k, :], start=(k == 0), stop=(k == ND - 1))
                        last.then_inc(s["proj_done"], 1)

                    def token_job(n, w, lo, hi, t):
                        out = bank_p(n)
                        for k in range(ND):
                            last = nc.tensor.matmul(out[:, 0:hi - lo], hT[:, k, t * P:(t + 1) * P], w[:, k, lo:hi],
                                                    start=(k == 0), stop=(k == ND - 1))
                        last.then_inc(s["proj_done"], 1)

                    def transpose_x(first):
                        for d in range(ND):
                            out = bank_p(first + d)
                            for t in range(NT):
                                last = nc.tensor.transpose(out[:, t * P:(t + 1) * P], xn[:, t, d * P:(d + 1) * P], ident)
                            last.then_inc(s["proj_done"], 1)

                    W = [view(slab[k % 3], ND, S) for k in range(3)]
                    pe.wait_ge(s["xn_ready"], NT)
                    transpose_x(J_HT)
                    pe.wait_ge(s["proj_free"], ND)
                    wait_slab(0)
                    for t in range(NT):
                        token_job(J_SGU + t, W[0], 0, S, t)
                    pe.wait_ge(s["bb_ready"], 1)
                    for J in range(2):
                        for ri in range(2):
                            last = nc.tensor.transpose(ps[:, BANK_T[0], (2 * J + ri) * P:(2 * J + ri + 1) * P],
                                                       bbar[:, ri, 4 * J:4 * J + 4, :].rearrange("p a b -> p (a b)"), ident)
                    last.then_inc(s["bb_done"], 1)
                    wait_slab(1)
                    for c in range(2):
                        feature_job(J_S5 + c, W[1], c * P)
                    pe.wait_ge(s["vn_ready"], NT)
                    pe.wait_ge(s["sgu_w_ready"], 1)
                    for g in range(SG):
                        last = nc.tensor.matmul(ps[:, BANK_S[g // 2], (g % 2) * 256:(g % 2 + 1) * 256], sgu_w[:, g, :],
                                                vn[:, :, g * 64:(g + 1) * 64], start=True, stop=True)
                        last.then_inc(s["mixed_done"], 1)
                    for c in range(2):
                        feature_job(J_KC + c, W[1], 256 + c * P)
                    pe.wait_ge(s["mixed_evac"], SG)
                    pe.wait_ge(s["bb_evac"], 1)
                    for c in range(2):
                        for t in range(NT):
                            last = nc.tensor.transpose(ps[:, BANK_T[c], t * P:(t + 1) * P], ys[:, t, c * P:(c + 1) * P], ident)
                        last.then_inc(s["ysT_done"], 1)

                    def s5_input(j):
                        J, r = j // 4, 32 * (j % 4)
                        if j == 0:
                            pe.wait_ge(s["proj_free"], J_S5 + 2)
                        else:
                            pe.wait_ge(s["twist_read"], j)
                        for ri in range(2):
                            last = nc.tensor.matmul(ps[:, BANK_S[ri], :], bbT[r:r + 32, J, ri, :], xsT[r:r + 32, J, :],
                                                    start=True, stop=True, tile_position=(r, 0))
                        last.then_inc(s["bu_done"], 1)

                    def s5_output(j):
                        J, r = j // 4, 32 * (j % 4)
                        if j == 0:
                            pe.wait_ge(s["cglu_in"], 16)
                        pe.wait_ge(s["h_ready"], j + 1)
                        for ri in range(2):
                            last = nc.tensor.matmul(ps[r:r + 32, BANK_O[J], :], cc[:, ri, j, :], s5_ab[j % 2][ri],
                                                    start=(ri == 0), stop=(ri == 1), tile_position=(0, r))
                        last.then_inc(s["y_done"], 1)

                    def rotate(n):
                        pe.wait_ge(s["proj_free"], J_KS + n + 1)
                        if n < 2:
                            pe.wait_ge(s["ysT_evac"], 2)
                        else:
                            pe.wait_ge(s["rope_done"], n - 1)
                        raw = q_rot[:, n, :] if n < 2 else q_plain[:, n - 2, :]
                        nc.tensor.matmul(ps[:, BANK_T[n % 2], :], rot, raw, start=True, stop=True).then_inc(s["rot_done"], 1)

                    def hidden(i):
                        wait_slab(4 + i)
                        w = view(slab[(4 + i) % 3], 32, P)
                        pe.wait_ge(s["rope_done"], 5 + i)
                        for l in range(32):
                            last = nc.tensor.matmul(ps[:, BANK_T[i], 0:93].rearrange("p (a b) -> p a b", a=3), w[:, l, :],
                                                    c_in[i][:, :, l:l + 16 * 30 + 1:16], start=(l == 0), stop=(l == 31))
                        last.then_inc(s["hidden_done"], 1)

                    units = {0: [0], 1: [1], 2: [2], 3: [3], 4: [4], 5: [5]}
                    for u in range(10):
                        if u < NCH:
                            s5_input(u)
                        if u < 6:
                            if u in (0, 4):
                                wait_slab(2 + u // 4)
                            feature_job(J_KS + u, W[2 if u < 4 else 0], (u % 4) * P)
                        elif u == 6:
                            for t in range(2):
                                token_job(J_V + t, W[0], 256, S, t)
                        elif u == 7:
                            for t in range(2, NT):
                                token_job(J_V + t, W[0], 256, S, t)
                            out = bank_p(J_NSA)
                            for t in range(NT):
                                for k in range(ND):
                                    last = nc.tensor.matmul(out[:, t * 24:(t + 1) * 24], hT[:, k, t * P:(t + 1) * P], wnsa[:, k, :],
                                                            start=(k == 0), stop=(k == ND - 1))
                            last.then_inc(s["proj_done"], 1)
                        elif u == 8:
                            pe.wait_ge(s["planes_clear"], 4)
                            hidden(0)
                        else:
                            hidden(1)
                        if 1 <= u <= 6:
                            rotate(u - 1)
                        if 1 <= u <= NCH:
                            s5_output(u - 1)

                    filled = [0]

                    def fill(m):
                        for _ in range(m):
                            if filled[0] >= 24 * ND:
                                return
                            n, k = divmod(filled[0], ND)
                            if k == 0:
                                if n % 4 == 0:
                                    wait_slab(6 + n // 4)
                                fill.out = bank_p(J_GATE + n)
                            w = view(slab[(6 + n // 4) % 3], ND, S)
                            last = nc.tensor.matmul(fill.out, w[:, k, (n % 4) * P:(n % 4 + 1) * P], hT[:, k, :],
                                                    start=(k == 0), stop=(k == ND - 1))
                            if k == ND - 1:
                                last.then_inc(s["proj_done"], 1)
                            filled[0] += 1

                    fill(4)
                    pe.wait_ge(s["gelu_done"], 2)
                    for m in range(2):
                        for k in range(2):
                            last = nc.tensor.matmul(ps[:, BANK_S[m], :], glu_w[:, k, m * P:(m + 1) * P], xsT[:, k, :],
                                                    start=(k == 0), stop=(k == 1))
                        last.then_inc(s["glu_done"], 1)
                    pe.wait_ge(s["hid_ready"], 2)
                    nc.tensor.matmul(ps[:, BANK_T[0], 0:64], small["w2k"], k_hid.rearrange("p a b -> p (a b)"),
                                     start=True, stop=True)
                    for g in range(G):
                        last = nc.tensor.matmul(ps[:, BANK_T[1], g * 64:(g + 1) * 64],
                                                v_hid[:, g].rearrange("p a b -> p (a b)"), small["w2v"],
                                                start=True, stop=True)
                    last.then_inc(s["ckv_done"], 1)
                    fill(8)
                    pe.wait_ge(s["ckv_ready"], 1)
                    pe.wait_ge(s["glu_read"], 2)
                    for t in range(NT):
                        for h in range(H):
                            col = (t % 2) * 256 + h * 32
                            last = nc.tensor.matmul(ps[:, BANK_S[t // 2], col:col + 32], q_plain[:, h % 4, t * P:(t + 1) * P],
                                                    k_cmp[:, h // 4, :], start=True, stop=True)
                    last.then_inc(s["cs_done"], 1)
                    fill(12)
                    pe.wait_ge(s["cp_ready"], 1)
                    for b in range(2):
                        for i in range(4):
                            t, g = 2 * b + i // 2, i % 2
                            last = nc.tensor.transpose(ps[:, BANK_T[b], i * P:(i + 1) * P],
                                                       c_sc[:, t, g * R:(g + 1) * R, :].rearrange("p a b -> p (a b)"), ident)
                        last.then_inc(s["ct_done"], 1)
                    fill(3)
                    for t in range(NT):
                        pe.wait_ge(s["ct_evac"], t // 2 + 1)
                        if t >= 2:
                            pe.wait_ge(s["oc_evac"], t - 1)
                        for g in range(G):
                            i = (t % 2) * 2 + g
                            last = nc.tensor.matmul(ps[:, BANK_O[t % 2], g * 256:(g + 1) * 256],
                                                    probT[t // 2][:, i * P:(i + 1) * P], v_cmp[:, g, :], start=True, stop=True)
                        last.then_inc(s["oc_done"], 1)

                    pe.wait_ge(s["rope_done"], 6)
                    pe.wait_ge(s["oc_evac"], NT)

                    def step_of(i):
                        return i // 32, (i // 8) % NT, i % 8

                    def scores(i):
                        br, t, h = step_of(i)
                        n = (t + 1) * P
                        if i >= 2:
                            pe.wait_ge(s["exp_done"], i - 1)
                        keys = (k_sel, k_win)[br]
                        out = ps[:, BANK_S[i % 2], 0:n]
                        nc.tensor.matmul(out, q_rot[:, h % 4, t * P:(t + 1) * P], keys[:, h // 4, 0:n], start=True, stop=False)
                        nc.tensor.matmul(out[:, t * P:n], ident, causal, start=False, stop=True).then_inc(s["scores_done"], 1)

                    def transposes(i):
                        t = step_of(i)[1]
                        pe.wait_ge(s["exp_done"], i + 1)
                        if i >= 2:
                            pe.wait_ge(s["pt_evac"], i - 1)
                        for b in range(t + 1):
                            last = nc.tensor.transpose(ps[:, BANK_T[i % 2], b * P:(b + 1) * P], prob[i % 2][:, b * P:(b + 1) * P], ident)
                        last.then_inc(s["tr_done"], 1)

                    def values(i):
                        br, t, h = step_of(i)
                        k = i // 8
                        pe.wait_ge(s["pt_evac"], i + 1)
                        if h == 0 and k >= 2:
                            pe.wait_ge(s["o_evac"], k - 1)
                        c0 = br * P + (h // 4) * DH
                        for b in range(t + 1):
                            last = nc.tensor.matmul(ps[:, BANK_O[k % 2], h * DH:(h + 1) * DH], probT[i % 2][:, b * P:(b + 1) * P],
                                                    v_tok[:, b, c0:c0 + DH], start=(b == 0), stop=(b == t))
                        last.then_inc(s["pv_done"], 1)

                    for i in range(N_ATT + 2):
                        if i < N_ATT:
                            scores(i)
                        fill(3)
                        if 1 <= i <= N_ATT:
                            transposes(i - 1)
                        if i >= 2:
                            values(i - 2)
                    fill(24 * ND)

                    pe.wait_ge(s["o_evac"], 8)
                    pe.wait_ge(s["pt_evac"], N_ATT)
                    for c in range(4):
                        if c >= 2:
                            pe.wait_ge(s["oT_evac"], c - 1)
                        for t in range(NT):
                            last = nc.tensor.transpose(ps[:, BANK_T[c % 2], t * P:(t + 1) * P], oacc[:, t, c * P:(c + 1) * P], ident)
                        last.then_inc(s["oT_done"], 1)
                    wait_slab(12)
                    wait_slab(13)
                    pe.wait_ge(s["oT_evac"], 4)
                    pe.wait_ge(s["exp_done"], N_ATT)
                    pe.wait_ge(s["s5_done"], 2)
                    wa = view(slab[12 % 3], 4, D)
                    wb = view(slab[13 % 3], 4, D)
                    for n in range(ND):
                        if n >= 2:
                            pe.wait_ge(s["merge_done"], n - 1)
                        for bank, w, k0, src, nk in ((BANK_S, wa, 0, oT, 4), (BANK_T, wb, 0, ysT, 2), (BANK_O, wb, 2, s5T, 2)):
                            for k in range(nk):
                                last = nc.tensor.matmul(ps[:, bank[n % 2], :], w[:, k0 + k, n * P:(n + 1) * P], src[:, k, :],
                                                        start=(k == 0), stop=(k == nk - 1))
                        last.then_inc(s["outp_done"], 1)
                    pe.wait_ge(s["merge_done"], ND)
                    for m in range(8):
                        half, t = divmod(m, NT)
                        if t == 0:
                            wait_slab(14 + half)
                        token_job(J_MIX + m, view(slab[(14 + half) % 3], ND, S), 0, S, t)
                    pe.wait_ge(s["xn_ready"], 2 * NT)
                    transpose_x(J_H2)
                    pe.wait_ge(s["proj_free"], J_END)
                    pe.wait_ge(s["router_in"], 16)
                    for t in range(NT):
                        for k in range(ND):
                            last = nc.tensor.matmul(ps[:, BANK_S[0], t * 36:(t + 1) * 36], hT[:, k, t * P:(t + 1) * P], rw[:, k, :],
                                                    start=(k == 0), stop=(k == ND - 1))
                    last.then_inc(s["rt_done"], 1)
                    pe.wait_ge(s["sel_ready"], 1)
                    for t in range(NT):
                        for j in range(t):
                            nc.tensor.matmul(ps[:, BANK_T[0], t * 32:(t + 1) * 32], ones, sel_all[:, j, :], start=(j == 0), stop=False)
                        nc.tensor.matmul(ps[:, BANK_T[0], t * 32:(t + 1) * 32], tri, sel_all[:, t, :], start=(t == 0), stop=True)
                    for t in range(NT):
                        last = nc.tensor.matmul(ps[:, BANK_T[1], 0:32], ones, sel_all[:, t, :], start=(t == 0), stop=(t == NT - 1))
                    last.then_inc(s["rank_done"], 1)

                    pe.sem_inc(s["x_gathered"], CRED)
                    pe.sem_inc(s["gu_done"], CRED)
                    pe.sem_inc(s["hT_done"], CRED)
                    pe.sem_inc(s["down_done"], CRED)
                    pe.wait_ge(s["sel_built"], 1 + CRED)
                    pe.wait_ge(s["route_done"], 1)
                    expert_gather(nc, ps, 2, xn, selm[0]).then_inc(s["x_gathered"], 1)
                    with pe.Fori(0, N_EXP // 2) as i:
                        for b in range(2):
                            e = 2 * i + b
                            pe.wait_ge(s["xe_ready"], e + 1 + CRED)
                            pe.wait_ge(s["hid_done"], e - 1 + CRED)
                            pe.wait_ge(w_in_sem[b][0], 16 * i + 16)
                            pe.wait_ge(w_in_sem[b][1], 16 * i + 16)
                            expert_gate_up(nc, ps, b, xeT[b], w_gate[b], w_up[b]).then_inc(s["gu_done"], 1)
                            pe.wait_ge(s["sel_built"], e + 2 + CRED)
                            pe.wait_ge(s["xe_ready"], e + CRED)
                            expert_gather(nc, ps, 2 + (1 - b), xn, selm[1 - b]).then_inc(s["x_gathered"], 1)
                            pe.wait_ge(s["hid_done"], e + 1 + CRED)
                            pe.wait_ge(s["hT_read"], e + CRED)
                            expert_transpose(nc, ps, hid, ident).then_inc(s["hT_done"], 1)
                            pe.wait_ge(s["hT_read"], e + 1 + CRED)
                            pe.wait_ge(w_in_sem[b][2], 16 * i + 16)
                            pe.wait_ge(s["y_read"], e - 1 + CRED)
                            expert_down(nc, ps, 6 + b, hidT[b], w_down[b]).then_inc(s["down_done"], 1)

                @block.scalar
                def _(act):
                    n = [0]

                    def link(ins):
                        ins.then_inc(s["chain_act"], 1)
                        n[0] += 1
                        act.wait_ge(s["chain_act"], n[0])

                    def evac(job, ops):
                        act.wait_ge(s["proj_done"], job + 1)
                        for k, (out, src, func, kw) in enumerate(ops):
                            ins = nc.scalar.activation(out, src, func, **kw)
                            if k < len(ops) - 1:
                                link(ins)
                        ins.then_inc(s["proj_free"], 1)

                    def bank(job):
                        return ps[:, BANK_P[job % 2], :]

                    def sum_squares():
                        for t in range(NT):
                            ins = nc.scalar.activation(xn[:, t, :], x[:, t, :], ACT.Square, accum_out=sumsq[:, t:t + 1])
                            if t < NT - 1:
                                link(ins)
                        ins.then_inc(s["sumsq_ready"], 1)

                    act.wait_ge(s["small_in"], 16)
                    step = s5_small[0]
                    act.wait_ge(s["bparam_in"], 16)
                    nc.scalar.activation(step, small["lstep"], ACT.Exp).then_inc(s["step_ready"], 1)
                    sum_squares()
                    act.wait_ge(s["lam_ready"], 1)
                    nc.scalar.activation(mag, s5_small[2], ACT.Exp).then_inc(s["mag_ready"], 1)
                    act.wait_ge(s["var_ready"], 1)
                    nc.scalar.activation(rstd, sumsq, ACT.Sqrt).then_inc(s["sd_ready"], 1)
                    act.wait_ge(s["angle_ready"], 1)
                    link(nc.scalar.activation(sin1, sincos[2], ACT.Sin))
                    nc.scalar.activation(cos1, sincos[3], ACT.Sin).then_inc(s["sincos_ready"], 1)
                    for d in range(ND):
                        evac(J_HT + d, [(hT[:, d, :], bank(J_HT + d), ACT.Identity, dict(scale=small["gmix"][:, d:d + 1]))])
                    for t in range(NT):
                        evac(J_SGU + t, [(z[:, t, :], bank(J_SGU + t), ACT.Gelu_apprx_tanh, {})])
                    act.wait_ge(s["proj_free"], J_SGU + NT)
                    for t in range(NT):
                        ins = nc.scalar.activation(vn[:, t, :], z[:, t, 256:512], ACT.Square, accum_out=vsumsq[:, t:t + 1])
                        if t < NT - 1:
                            link(ins)
                    ins.then_inc(s["vsq_ready"], 1)
                    act.wait_ge(s["vvar_ready"], 1)
                    nc.scalar.activation(vrstd, vsumsq, ACT.Sqrt).then_inc(s["vsd_ready"], 1)
                    for c in range(2):
                        evac(J_S5 + c, [(xsT[:, c, :], bank(J_S5 + c), ACT.Identity, {})])
                    act.wait_ge(s["planes_clear"], 2)
                    for c in range(2):
                        b = bank(J_KC + c)
                        evac(J_KC + c, [(c_in[c][0:64, 0, :], b[0:64], ACT.Identity, {}), (c_in[c][64:P, 1, :], b[64:P], ACT.Identity, {})])
                    for i in range(2):
                        evac(J_KS + i, [(q_rot[:, i, :], bank(J_KS + i), ACT.Identity, {})])
                    for i in range(4):
                        evac(J_Q + i, [(q_plain[:, i, :], bank(J_Q + i), ACT.Identity, dict(scale=DH ** -0.5))])
                    for t in range(NT):
                        evac(J_V + t, [(v_tok[:, t, :], bank(J_V + t)[:, 0:256], ACT.Identity, {})])
                    evac(J_NSA, [(nsa_g, bank(J_NSA)[:, 0:96].rearrange("p (a b) -> p a b", a=NT), ACT.Tanh, dict(scale=0.5))])
                    for c in range(2):
                        act.wait_ge(s["y1_ready"], c + 1)
                        nc.scalar.activation(xsT[:, c, :], xsT[:, c, :], ACT.Gelu_apprx_tanh).then_inc(s["gelu_done"], 1)
                    act.wait_ge(s["hidden_done"], 2)
                    for i in range(2):
                        link(nc.scalar.activation(c_bias[:, i:i + 1], ps[:, BANK_T[i], 62:63], ACT.Identity))
                    act.wait_ge(s["planes_clear"], 5)
                    src = [ps[:, BANK_T[i], 0:62].rearrange("p (a b) -> p a b", a=2) for i in range(2)]
                    nc.scalar.activation(k_hid[:, :, 0:31], src[0], ACT.Gelu_apprx_tanh, bias=c_bias[:, 0:1]).then_inc(s["hid_ready"], 1)
                    nc.scalar.activation(v_hid[:, :, :, 0:31], src[1].unsqueeze(2).to_broadcast([P, G, R, 31]),
                                         ACT.Gelu_apprx_tanh, bias=c_bias[:, 1:2]).then_inc(s["hid_ready"], 1)
                    for m in range(2):
                        act.wait_ge(s["glu_done"], m + 1)
                        nc.scalar.activation(s5T[:, m, :], ps[:, BANK_S[m], :], ACT.Tanh, scale=0.5,
                                             bias=glub_h[:, m:m + 1]).then_inc(s["glu_read"], 1)
                    act.wait_ge(s["h_ready"], NCH)
                    got = [0]

                    def gate(upto):
                        while got[0] < min(upto, 24):
                            j = J_GATE + got[0]
                            evac(j, [(gates[:, got[0], :], bank(j), ACT.Tanh, dict(scale=0.5))])
                            got[0] += 1

                    gate((4 + 8) // ND)
                    act.wait_ge(s["cexp_in"], 1)
                    nc.scalar.activation(c_scf, c_scf, ACT.Exp).then_inc(s["cexp_done"], 1)
                    before = 4 + 8 + 12 + 3
                    gate(before // ND)
                    for i in range(N_ATT):
                        t = (i // 8) % NT
                        nk = (t + 1) * P
                        act.wait_ge(s["max_done"], i + 1)
                        if i >= 2:
                            act.wait_ge(s["tr_done"], i - 1)
                        else:
                            act.wait_ge(s["ct_done"], 2)
                        nc.scalar.activation(prob[i % 2][:, 0:nk], ps[:, BANK_S[i % 2], 0:nk], ACT.Exp, bias=rowmax[:, i % 4:i % 4 + 1],
                                             accum_out=rowsum[:, i:i + 1]).then_inc(s["exp_done"], 1)
                        gate((before + 3 * (i + 1)) // ND)
                    gate(24)
                    act.wait_ge(s["proj_free"], J_H2)
                    sum_squares()
                    act.wait_ge(s["var_ready"], 2)
                    nc.scalar.activation(rstd, sumsq, ACT.Sqrt).then_inc(s["sd_ready"], 1)
                    for d in range(ND):
                        evac(J_H2 + d, [(hT[:, d, :], bank(J_H2 + d), ACT.Identity, dict(scale=small["gffn"][:, d:d + 1]))])
                    act.wait_ge(s["gexp_in"], 1)
                    nc.scalar.activation(gtmp, gtmp, ACT.Exp).then_inc(s["gexp_done"], 1)
                    act.wait_ge(s["e2_in"], 1)
                    nc.scalar.activation(r1[4], r1[4], ACT.Exp).then_inc(s["e2_done"], 1)
                    act.sem_inc(s["silu_done"], CRED)
                    act.sem_inc(s["hT_read"], CRED)
                    act.sem_inc(s["y_read"], CRED)
                    act.sem_inc(y_out[0], 1)
                    act.sem_inc(y_out[1], 1)
                    act.wait_ge(s["route_done"], 1)
                    with act.Fori(0, N_EXP // 2) as i:
                        for b in range(2):
                            e = 2 * i + b
                            act.wait_ge(s["gu_done"], e + 1 + CRED)
                            act.wait_ge(s["hid_done"], e + CRED)
                            nc.scalar.activation(silu[0:64], ps[0:64, b, :], ACT.Silu).then_inc(s["silu_done"], 1)
                            act.wait_ge(s["hT_done"], e + 1 + CRED)
                            act.wait_ge(s["down_done"], e - 1 + CRED)
                            nc.scalar.activation(hidT[b].rearrange("p a b -> p (a b)"), ps[:, 4, 0:256],
                                                 ACT.Identity).then_inc(s["hT_read"], 1)
                            act.wait_ge(s["down_done"], e + 1 + CRED)
                            act.wait_ge(y_out[b], 32 * i + 1)
                            nc.scalar.activation(ybuf[b], ps[:, 6 + b, :], ACT.Identity).then_inc(s["y_read"], 1)
                            act.wait_ge(s["y_read"], e + 1 + CRED)
                            for half in range(2):
                                act.dma_start(io["ybuf"][bass.ds(e * CAP, CAP), half * 512:(half + 1) * 512],
                                              ybuf[b][64 * half:64 * half + 64, :]).then_inc(y_out[b], 16)
                    for b in range(2):
                        act.wait_ge(y_out[b], 32 * (N_EXP // 2) + 1)

                @block.vector
                def _(dve):
                    n = [0]
                    v = nc.vector

                    def link(ins):
                        ins.then_inc(s["chain_dve"], 1)
                        n[0] += 1
                        dve.wait_ge(s["chain_dve"], n[0])

                    told = {}

                    def tell(ins, name):
                        ins.then_inc(s[name], 1)
                        told[name] = told.get(name, 0) + 1
                        dve.wait_ge(s[name], told[name])

                    def normalise(k):
                        dve.wait_ge(s["sumsq_ready"], k)
                        tell(v.tensor_scalar(sumsq, sumsq, 1.0 / D, EPS, ALU.mult, ALU.add), "var_ready")
                        if k == 1:
                            s5_angles()
                        dve.wait_ge(s["sd_ready"], k)
                        link(v.reciprocal(rstd, rstd))
                        for t in range(NT):
                            tell(v.tensor_scalar(xn[:, t, :], x[:, t, :], rstd[:, t:t + 1], None, ALU.mult), "xn_ready")

                    _, theta, lam, den, nr, cre, cim, u1, u2, abr, abi = s5_small[:11]

                    def s5_angles():
                        reduce_angle(nc, link, theta, sincos[1], sincos[2], sincos[3])
                        tell(v.tensor_scalar(glub_h, small["glub"], 0.5, None, ALU.mult), "angle_ready")

                    dve.wait_ge(s["step_ready"], 1)
                    link(v.tensor_tensor(theta, small["a_im"], s5_small[0], ALU.mult))
                    tell(v.tensor_tensor(lam, small["a_re"], s5_small[0], ALU.mult), "lam_ready")
                    normalise(1)
                    dve.wait_ge(s["mag_ready"], 1)
                    dve.wait_ge(s["sincos_ready"], 1)
                    dve.wait_ge(s["bparam_in"], 16)
                    link(v.tensor_tensor(abr, mag, cos1, ALU.mult))
                    link(v.tensor_tensor(abi, mag, sin1, ALU.mult))
                    link(v.tensor_scalar(nr, abr, -1.0, None, ALU.add))
                    link(v.tensor_tensor(u1, small["a_re"], small["a_re"], ALU.mult))
                    link(v.tensor_tensor(u2, small["a_im"], small["a_im"], ALU.mult))
                    link(v.tensor_tensor(den, u1, u2, ALU.add))
                    link(v.reciprocal(den, den))
                    link(v.tensor_tensor(u1, nr, small["a_re"], ALU.mult))
                    link(v.tensor_tensor(u2, abi, small["a_im"], ALU.mult))
                    link(v.tensor_tensor(cre, u1, u2, ALU.add))
                    link(v.tensor_tensor(cre, cre, den, ALU.mult))
                    link(v.tensor_tensor(u1, abi, small["a_re"], ALU.mult))
                    link(v.tensor_tensor(u2, nr, small["a_im"], ALU.mult))
                    link(v.tensor_tensor(cim, u1, u2, ALU.subtract))
                    link(v.tensor_tensor(cim, cim, den, ALU.mult))
                    cre_b = cre.unsqueeze(2).to_broadcast([P, NCH, 32])
                    cim_b = cim.unsqueeze(2).to_broadcast([P, NCH, 32])
                    link(v.tensor_tensor(bbar[:, 0], b_in[:, 0], cre_b, ALU.mult))
                    link(v.tensor_tensor(bb_tmp, b_in[:, 1], cim_b, ALU.mult))
                    link(v.tensor_tensor(bbar[:, 0], bbar[:, 0], bb_tmp, ALU.subtract))
                    link(v.tensor_tensor(bbar[:, 1], b_in[:, 1], cre_b, ALU.mult))
                    link(v.tensor_tensor(bb_tmp, b_in[:, 0], cim_b, ALU.mult))
                    tell(v.tensor_tensor(bbar[:, 1], bbar[:, 1], bb_tmp, ALU.add), "bb_ready")
                    dve.wait_ge(s["bb_done"], 1)
                    tell(v.tensor_copy(view(O_BBT, 512), ps[:, BANK_T[0], :]), "bb_evac")

                    dve.wait_ge(s["vsq_ready"], 1)
                    tell(v.tensor_scalar(vsumsq, vsumsq, 1.0 / 256, EPS, ALU.mult, ALU.add), "vvar_ready")
                    dve.wait_ge(s["vsd_ready"], 1)
                    link(v.reciprocal(vrstd, vrstd))
                    dve.wait_ge(s["sgu_in"], 16)
                    for t in range(NT):
                        tell(v.scalar_tensor_tensor(vn[:, t, :], z[:, t, 256:512], vrstd[:, t:t + 1], sgu_g, ALU.mult, ALU.mult), "vn_ready")
                    for g in range(SG):
                        if g % 2 == 0:
                            dve.wait_ge(s["mixed_done"], g + 2)
                        src = ps[:, BANK_S[g // 2], (g % 2) * 256:(g % 2 + 1) * 256].rearrange("p (a b) -> p a b", a=NT)
                        tell(v.scalar_tensor_tensor(ys[:, :, g * 64:(g + 1) * 64], src, small["sgub"][:, g:g + 1],
                                                    z[:, :, g * 64:(g + 1) * 64], ALU.add, ALU.mult), "mixed_evac")
                    for c in range(2):
                        dve.wait_ge(s["ysT_done"], c + 1)
                        tell(v.tensor_copy(ysT[:, c, :], ps[:, BANK_T[c], :]), "ysT_evac")

                    def s5_chunk(j):
                        a, b = s5_ab[j % 2]
                        c, d = s5_c, s5_d
                        cos, sin = tab_re[:, j, :], tab_im[:, j, :]
                        re, im = ps[:, BANK_S[0], :], ps[:, BANK_S[1], :]
                        dve.wait_ge(s["bu_done"], j + 1)
                        if j >= 2:
                            dve.wait_ge(s["y_done"], j - 1)
                        link(v.tensor_tensor(a, re, cos, ALU.mult))
                        link(v.tensor_tensor(c, im, sin, ALU.mult))
                        link(v.tensor_tensor(a, a, c, ALU.add))
                        link(v.tensor_tensor(b, im, cos, ALU.mult))
                        tell(v.tensor_tensor(c, re, sin, ALU.mult), "twist_read")
                        link(v.tensor_tensor(b, b, c, ALU.subtract))
                        m = mag[:, j:j + 1].to_broadcast([P, S])
                        link(v.tensor_tensor_scan(c, m, a, 0.0, ALU.mult, ALU.add))
                        link(v.tensor_tensor_scan(d, m, b, 0.0, ALU.mult, ALU.add))
                        link(v.tensor_tensor(a, c, cos, ALU.mult))
                        link(v.tensor_tensor(b, d, sin, ALU.mult))
                        link(v.tensor_tensor(a, a, b, ALU.subtract))
                        link(v.tensor_tensor(b, d, cos, ALU.mult))
                        link(v.tensor_tensor(c, c, sin, ALU.mult))
                        tell(v.scalar_tensor_tensor(b, b, -1.0, c, ALU.mult, ALU.subtract), "h_ready")

                    def rope(i):
                        dve.wait_ge(s["rot_done"], i + 1)
                        part = ps[:, BANK_T[i % 2], :]
                        c, d = s5_c, s5_d
                        raw = q_rot[:, i, :] if i < 2 else q_plain[:, i - 2, :]
                        link(v.tensor_tensor(c, part, rope_sin, ALU.mult))
                        link(v.tensor_tensor(d, raw, rope_cos, ALU.mult))
                        if i < 2:
                            planes = (k_sel, k_win)[i]
                            dve.wait_ge(s["planes_clear"], 4)
                            link(v.tensor_tensor(planes[0:64, 0, :], c[0:64], d[0:64], ALU.add))
                            tell(v.tensor_tensor(planes[64:P, 1, :], c[64:P], d[64:P], ALU.add), "rope_done")
                        else:
                            tell(v.tensor_tensor(q_rot[:, i - 2, :], c, d, ALU.add), "rope_done")

                    dve.wait_ge(s["table_ready"], 1)
                    for u in range(NCH):
                        s5_chunk(u)
                        if 1 <= u <= 6:
                            rope(u - 1)
                    for c in range(2):
                        dve.wait_ge(s["y_done"], 4 * (c + 1))
                        tell(v.scalar_tensor_tensor(xsT[:, c, :], xsT[:, c, :], small["d"][:, c:c + 1], ps[:, BANK_O[c], :],
                                                    ALU.mult, ALU.add), "y1_ready")
                    dve.wait_ge(s["proj_free"], J_NSA + 1)
                    link(v.tensor_scalar(nsa_g, nsa_g, 1.0, 0.5, ALU.add, ALU.mult))
                    dve.wait_ge(s["hidden_done"], 2)
                    dve.wait_ge(s["planes_clear"], 5)
                    dve.wait_ge(s["ckv_done"], 1)
                    link(v.tensor_copy(k_cmp[0:64, 0, :], ps[0:64, BANK_T[0], 0:32]))
                    link(v.tensor_copy(k_cmp[64:P, 1, :], ps[64:P, BANK_T[0], 32:64]))
                    for r in range(R):
                        ins = v.tensor_copy(v_cmp[32 * r:32 * r + 32, :, r * DH:(r + 1) * DH],
                                            ps[32 * r:32 * r + 32, BANK_T[1], 0:P].rearrange("p (a b) -> p a b", a=2))
                        if r < R - 1:
                            link(ins)
                    tell(ins, "ckv_ready")
                    for m in range(2):
                        dve.wait_ge(s["glu_read"], m + 1)
                        link(v.tensor_scalar(s5T[:, m, :], s5T[:, m, :], 1.0, 0.5, ALU.add, ALU.mult))
                        tell(v.tensor_tensor(s5T[:, m, :], s5T[:, m, :], xsT[:, m, :], ALU.mult), "s5_done")
                    dve.wait_ge(s["cs_done"], 1)
                    dve.wait_ge(s["y_done"], NCH)
                    for b in range(2):
                        src = ps[:, BANK_S[b], :].rearrange("p (t h c) -> p t h c", t=2, h=H)
                        ins = v.tensor_tensor(c_sc[:, 2 * b:2 * b + 2], src,
                                              c_add[:, 2 * b:2 * b + 2, :].unsqueeze(2).to_broadcast([P, 2, H, 32]), ALU.add)
                        if b == 0:
                            link(ins)
                    tell(ins, "cs_read")
                    link(v.tensor_reduce(c_max, c_scf, AX, ALU.max))
                    tell(v.tensor_tensor(c_scf, c_scf, c_max.unsqueeze(2).to_broadcast([P, 32, 32]), ALU.subtract), "cexp_in")
                    dve.wait_ge(s["cexp_done"], 1)
                    link(v.tensor_tensor(c_sc, c_sc, c_01.unsqueeze(2).to_broadcast([P, NT, H, 32]), ALU.mult))
                    link(v.tensor_reduce(c_sum, c_scf, AX, ALU.add))
                    link(v.tensor_scalar(c_sum, c_sum, 1e-30, None, ALU.max))
                    link(v.reciprocal(c_sum, c_sum))
                    link(v.tensor_tensor(c_sum.rearrange("p (t h) -> p t h", t=NT), c_sum.rearrange("p (t h) -> p t h", t=NT),
                                         nsa_g[:, :, 0:24:3], ALU.mult))
                    tell(v.tensor_tensor(c_scf, c_scf, c_sum.unsqueeze(2).to_broadcast([P, 32, 32]), ALU.mult), "cp_ready")
                    for b in range(2):
                        dve.wait_ge(s["ct_done"], b + 1)
                        tell(v.tensor_copy(probT[b], ps[:, BANK_T[b], :]), "ct_evac")
                    dve.wait_ge(s["glu_done"], 2)
                    for t in range(NT):
                        dve.wait_ge(s["oc_done"], t + 1)
                        tell(v.tensor_copy(oacc[:, t, :], ps[:, BANK_O[t % 2], :]), "oc_evac")

                    def out_of(k):
                        br, t = divmod(k, NT)
                        dve.wait_ge(s["pv_done"], 8 * k + 8)
                        link(v.reciprocal(rinv, rowsum[:, 8 * k:8 * k + 8]))
                        link(v.tensor_tensor(wgt, rinv, nsa_g[:, t, 1 + br:24:3], ALU.mult))
                        link(v.tensor_tensor(o_tmp.rearrange("p (h d) -> p h d", h=H),
                                             ps[:, BANK_O[k % 2], :].rearrange("p (h d) -> p h d", h=H),
                                             wgt.unsqueeze(2).to_broadcast([P, H, DH]), ALU.mult))
                        tell(v.tensor_tensor(oacc[:, t, :], oacc[:, t, :], o_tmp, ALU.add), "o_evac")

                    for i in range(N_ATT + 3):
                        if i < N_ATT:
                            nk = ((i // 8) % NT + 1) * P
                            dve.wait_ge(s["scores_done"], i + 1)
                            tell(v.tensor_reduce(rowmax[:, i % 4:i % 4 + 1], ps[:, BANK_S[i % 2], 0:nk], AX, ALU.max, negate=True), "max_done")
                        if 1 <= i <= N_ATT:
                            j = i - 1
                            nk = ((j // 8) % NT + 1) * P
                            dve.wait_ge(s["tr_done"], j + 1)
                            if j >= 2:
                                dve.wait_ge(s["pv_done"], j - 1)
                            tell(v.tensor_copy(probT[j % 2][:, 0:nk], ps[:, BANK_T[j % 2], 0:nk]), "pt_evac")
                        if i >= 3 and (i - 3) % 8 == 7:
                            out_of((i - 3) // 8)
                    for c in range(4):
                        dve.wait_ge(s["oT_done"], c + 1)
                        tell(v.tensor_copy(oT[:, c, :], ps[:, BANK_T[c % 2], :]), "oT_evac")
                    dve.wait_ge(s["proj_free"], J_GATE + 24)
                    m1, m2 = m_tmp
                    for c in range(ND):
                        dve.wait_ge(s["outp_done"], c + 1)
                        link(v.scalar_tensor_tensor(m1, gates[:, c, :], 1.0, ps[:, BANK_S[c % 2], :], ALU.add, ALU.mult))
                        link(v.scalar_tensor_tensor(m2, gates[:, ND + c, :], 1.0, ps[:, BANK_T[c % 2], :], ALU.add, ALU.mult))
                        link(v.tensor_tensor(m1, m1, m2, ALU.add))
                        link(v.scalar_tensor_tensor(m2, gates[:, 2 * ND + c, :], 1.0, ps[:, BANK_O[c % 2], :], ALU.add, ALU.mult))
                        tell(v.tensor_tensor(hT[:, c, :], m1, m2, ALU.add), "merge_done")
                    for m in range(8):
                        half, t = divmod(m, NT)
                        job = J_MIX + m
                        dve.wait_ge(s["proj_done"], job + 1)
                        xs = x[:, t, half * 512:(half + 1) * 512]
                        v.scalar_tensor_tensor(xs, ps[:, BANK_P[job % 2], :], 0.5, xs, ALU.mult, ALU.add).then_inc(s["proj_free"], 1)
                    dve.wait_ge(s["proj_free"], J_MIX + 8)
                    normalise(2)

                    dve.wait_ge(s["rt_done"], 1)
                    dve.wait_ge(s["router_in"], 16)
                    dve.wait_ge(s["mconst_in"], 16)
                    link(v.tensor_tensor(logit, ps[:, BANK_S[0], 0:144].rearrange("p (a b) -> p a b", a=NT),
                                         rb.unsqueeze(1).to_broadcast([P, NT, 36]), ALU.add))
                    gl = logit[:, :, 0:4]
                    el = logit[:, :, 4:36]

                    def one_hot(out, val, top, desc, w, tmp):
                        link(v.tensor_reduce(top, val, AX, ALU.max))
                        link(v.tensor_tensor(out, val, top.unsqueeze(2).to_broadcast([P, NT, w]), ALU.is_equal))
                        link(v.tensor_tensor(out, out, desc.unsqueeze(1).to_broadcast([P, NT, w]), ALU.mult))
                        link(v.tensor_reduce(tmp, out, AX, ALU.max))
                        link(v.tensor_tensor(out, out, tmp.unsqueeze(2).to_broadcast([P, NT, w]), ALU.is_equal))

                    gmax, gden, top1, top2, e2, first, den1, tmp4, d1, d2 = r1
                    one_hot(goh, gl, gmax, desc4, 4, first)
                    tell(v.tensor_tensor(gtmp, gl, gmax.unsqueeze(2).to_broadcast([P, NT, 4]), ALU.subtract), "gexp_in")
                    link(v.tensor_scalar(goh, goh, 1.0, -NEG, ALU.subtract, ALU.mult))
                    link(v.tensor_tensor(em.rearrange("p t (g e) -> p t g e", g=4), el.rearrange("p t (g e) -> p t g e", g=4),
                                         goh.unsqueeze(3).to_broadcast([P, NT, 4, E_PER]), ALU.add))
                    one_hot(oh[0], em, top1, desc32, 32, first)
                    link(v.scalar_tensor_tensor(em, oh[0], 2 * NEG, em, ALU.mult, ALU.add))
                    one_hot(oh[1], em, top2, desc32, 32, first)
                    tell(v.tensor_tensor(e2, top2, top1, ALU.subtract), "e2_in")
                    tell(v.tensor_tensor(sel_all, oh[0], oh[1], ALU.add), "sel_ready")
                    dve.wait_ge(s["gexp_done"], 1)
                    link(v.tensor_reduce(gden, gtmp, AX, ALU.add))
                    dve.wait_ge(s["e2_done"], 1)
                    link(v.tensor_scalar(den1, e2, 1.0, None, ALU.add))
                    link(v.tensor_tensor(den1, den1, gden, ALU.mult))
                    link(v.reciprocal(cw[0], den1))
                    link(v.tensor_tensor(cw[1], cw[0], e2, ALU.mult))
                    dve.wait_ge(s["rank_done"], 1)
                    link(v.tensor_copy(rank, ps[:, BANK_T[0], 0:P].rearrange("p (a b) -> p a b", a=NT)))
                    link(v.memset(slot[:, N_EXP, :], -1.0))
                    link(v.tensor_scalar(eq, rank, 1.0, None, ALU.add))
                    link(v.tensor_tensor(eq, eq, sel_all, ALU.mult))
                    link(v.tensor_scalar(slot[:, 0:N_EXP, :].rearrange("p e t -> p t e"), eq, -1.0, None, ALU.add))
                    link(v.tensor_scalar(eq, rank, float(CAP - 1), None, ALU.min))
                    link(v.tensor_tensor(eq, eq, base_e.unsqueeze(1).to_broadcast([P, NT, 32]), ALU.add))
                    link(v.tensor_scalar(rank, rank, float(CAP), None, ALU.is_lt))
                    for k, dk in ((0, d1), (1, d2)):
                        link(v.tensor_tensor(em, eq, oh[k], ALU.mult))
                        link(v.tensor_reduce(dk, em, AX, ALU.add))
                        link(v.tensor_copy(didx[k], dk))
                        link(v.tensor_tensor(em, rank, oh[k], ALU.mult))
                        link(v.tensor_reduce(dk, em, AX, ALU.add))
                        link(v.tensor_tensor(cwm[k], cw[k], dk, ALU.mult))
                    link(v.tensor_copy(countf[:, 0:N_EXP], ps[:, BANK_T[1], 0:N_EXP]))
                    link(v.tensor_reduce(countf[:, N_EXP:N_EXP + 1], ps[:, BANK_T[1], 0:N_EXP], AX, ALU.max))
                    tell(v.tensor_copy(counts, countf), "route_done")

                    dve.sem_inc(s["sel_built"], CRED)
                    dve.sem_inc(s["xe_ready"], CRED)
                    dve.sem_inc(s["hid_done"], CRED)
                    build_sel(0, 0).then_inc(s["sel_built"], 1)
                    dve.wait_ge(s["x_gathered"], 1 + CRED)
                    take_x(0, 2).then_inc(s["xe_ready"], 1)
                    with dve.Fori(0, N_EXP // 2) as i:
                        for b in range(2):
                            e = 2 * i + b
                            dve.wait_ge(s["x_gathered"], e + CRED)
                            dve.wait_ge(s["sel_built"], e + 1 + CRED)
                            build_sel(e + 1, 1 - b).then_inc(s["sel_built"], 1)
                            dve.wait_ge(s["silu_done"], e + 1 + CRED)
                            dve.wait_ge(s["gu_done"], e + 1 + CRED)
                            dve.wait_ge(s["hT_done"], e + CRED)
                            v.tensor_tensor(hid[0:64], ps[64:P, b, :], silu[0:64], ALU.mult).then_inc(s["hid_done"], 1)
                            dve.wait_ge(s["x_gathered"], e + 2 + CRED)
                            dve.wait_ge(s["gu_done"], e + CRED)
                            take_x(1 - b, 2 + (1 - b)).then_inc(s["xe_ready"], 1)

                @block.gpsimd
                def _(pool):
                    g = nc.gpsimd
                    n = [0]

                    def link(ins):
                        ins.then_inc(s["chain_pool"], 1)
                        n[0] += 1
                        pool.wait_ge(s["chain_pool"], n[0])

                    cleared = [0]

                    def clear_told(ins):
                        ins.then_inc(s["planes_clear"], 1)
                        cleared[0] += 1
                        pool.wait_ge(s["planes_clear"], cleared[0])

                    pool.wait_ge(s["small_in"], 16)
                    for i in range(2):
                        link(g.memset(c_in[i][64:P, 0, :], 0.0))
                        link(g.memset(c_in[i][0:64, 1, :], 0.0))
                        link(g.memset(c_in[i][:, 2, :], 0.0))
                        clear_told(g.tensor_copy(c_in[i][:, 2, 0:32], small["posk" if i == 0 else "posv"]))
                    for planes in (k_sel, k_win):
                        link(g.memset(planes[64:P, 0, :], 0.0))
                        clear_told(g.memset(planes[0:64, 1, :], 0.0))
                    pool.wait_ge(s["sgu_in"], 16)
                    g.affine_select(out=sgu_w, in_=sgu_w, compare_op=ALU.is_ge, fill=0.0, base=0,
                                    pattern=[[0, SG], [1, P]], channel_multiplier=-1).then_inc(s["sgu_w_ready"], 1)
                    pool.wait_ge(s["sgu_w_ready"], 1)
                    pool.wait_ge(s["sincos_ready"], 1)
                    link(g.memset(tab_re[:, :, 0], 1.0))
                    link(g.memset(tab_im[:, :, 0], 0.0))
                    pr, pi, qa, qb = pw
                    link(g.tensor_copy(pr, cos1))
                    link(g.tensor_copy(pi, sin1))
                    m = 1
                    while m < S:
                        t_ = view(tab_tmp, NCH, m)
                        prb = pr.unsqueeze(2).to_broadcast([P, NCH, m])
                        pib = pi.unsqueeze(2).to_broadcast([P, NCH, m])
                        re, im = tab_re[:, :, 0:m], tab_im[:, :, 0:m]
                        re2, im2 = tab_re[:, :, m:2 * m], tab_im[:, :, m:2 * m]
                        link(g.tensor_tensor(re2, re, prb, ALU.mult))
                        link(g.tensor_tensor(t_, im, pib, ALU.mult))
                        link(g.tensor_tensor(re2, re2, t_, ALU.subtract))
                        link(g.tensor_tensor(im2, re, pib, ALU.mult))
                        link(g.tensor_tensor(t_, im, prb, ALU.mult))
                        ins = g.tensor_tensor(im2, im2, t_, ALU.add)
                        m *= 2
                        if m < S:
                            link(ins)
                            link(g.tensor_tensor(qa, pr, pr, ALU.mult))
                            link(g.tensor_tensor(qb, pi, pi, ALU.mult))
                            link(g.tensor_tensor(pi, pi, pr, ALU.mult))
                            link(g.tensor_tensor(pi, pi, pi, ALU.add))
                            link(g.tensor_tensor(pr, qa, qb, ALU.subtract))
                    ins.then_inc(s["table_ready"], 1)
                    pool.wait_ge(s["table_ready"], 1)
                    pool.wait_ge(s["hidden_done"], 2)
                    link(g.memset(view(O_CW, 576), 0.0))
                    link(g.memset(k_hid[:, :, 31], 0.0))
                    g.memset(v_hid[:, :, :, 31], 0.0).then_inc(s["planes_clear"], 1)

            most = nc.values_load(counts[0:1, N_EXP:N_EXP + 1], min_val=0, max_val=S)
            with nc.If(most > CAP):
                nc.all_engine_barrier()
                with nc.Fori(1, S // CAP):
                    with nc.Block() as block:
                        @block.vector
                        def _(dve):
                            nc.vector.tensor_scalar(slot, slot, float(CAP), None, ALU.subtract).then_inc(so["ov_shift"], 1)
                            nc.vector.tensor_scalar(countf, countf, float(CAP), None, ALU.subtract).then_inc(so["ov_shift"], 1)
                            dve.wait_ge(so["ov_shift"], 2)
                            nc.vector.tensor_scalar(counts, countf, 0.0, None, ALU.max).then_inc(so["ov_shift"], 1)
                            dve.wait_ge(so["ov_shift"], 3)
                    clear(nc, over_sems)
                    with nc.Fori(0, N_EXP) as e:
                        left = nc.values_load(counts[0:1, bass.ds(e, 1)], min_val=0, max_val=S)
                        with nc.If(left > 0):
                            with nc.Block() as block:
                                @block.sync
                                def _(sp):
                                    for w, name, k in ((w_gate, "expert_w_gate", ND), (w_up, "expert_w_up", ND),
                                                       (w_down, "expert_w_down", NH)):
                                        sp.dma_start(w[0], expert_rows(io[name], e, k)).then_inc(so["ov_weights"], 16)
                                    sp.wait_ge(so["ov_weights"], 48)

                                @block.tensor
                                def _(pe):
                                    pe.wait_ge(so["ov_sel"], 1)
                                    expert_gather(nc, ps, 2, xn, selm[0]).then_inc(so["ov_gathered"], 1)
                                    pe.wait_ge(so["ov_xe"], 1)
                                    pe.wait_ge(so["ov_weights"], 48)
                                    expert_gate_up(nc, ps, 0, xeT[0], w_gate[0], w_up[0]).then_inc(so["ov_gu"], 1)
                                    pe.wait_ge(so["ov_selw"], 1)
                                    for t in range(NT):
                                        last = nc.tensor.transpose(ps[0:CAP, 5, t * P:(t + 1) * P], selm[1][:, t, :], ident)
                                    last.then_inc(so["ov_selT"], 1)
                                    pe.wait_ge(so["ov_hid"], 1)
                                    expert_transpose(nc, ps, hid, ident).then_inc(so["ov_hT"], 1)
                                    pe.wait_ge(so["ov_hT_read"], 1)
                                    for half in range(2):
                                        for k in range(NH):
                                            last = nc.tensor.matmul(ps[0:CAP, 6 + half, :], hidT[0][:, k, :],
                                                                    w_down[0][:, k, half * 512:(half + 1) * 512],
                                                                    start=(k == 0), stop=(k == NH - 1))
                                    last.then_inc(so["ov_down"], 1)
                                    pe.wait_ge(so["ov_selT_read"], 1)
                                    pe.wait_ge(so["ov_y"], 2)
                                    for t in range(NT):
                                        for half in range(2):
                                            nc.tensor.matmul(ps[:, 2 * t + half, :], silu[0:CAP, t * P:(t + 1) * P], ybuf[half][0:CAP, :],
                                                             start=True, stop=True).then_inc(so["ov_back"], 1)

                                @block.scalar
                                def _(act):
                                    act.wait_ge(so["ov_gu"], 1)
                                    nc.scalar.activation(silu[0:CAP], ps[0:CAP, 0, :], ACT.Silu).then_inc(so["ov_silu"], 1)
                                    act.wait_ge(so["ov_hT"], 1)
                                    nc.scalar.activation(hidT[0].rearrange("p a b -> p (a b)"), ps[:, 4, 0:256],
                                                         ACT.Identity).then_inc(so["ov_hT_read"], 1)
                                    act.wait_ge(so["ov_selT"], 1)
                                    act.wait_ge(so["ov_hid"], 1)
                                    nc.scalar.activation(silu[0:CAP], ps[0:CAP, 5, :], ACT.Identity).then_inc(so["ov_selT_read"], 1)
                                    act.wait_ge(so["ov_down"], 1)
                                    for half in range(2):
                                        nc.scalar.activation(ybuf[half][0:CAP], ps[0:CAP, 6 + half, :],
                                                             ACT.Identity).then_inc(so["ov_y"], 1)

                                @block.vector
                                def _(dve):
                                    v = nc.vector
                                    build_sel(e, 0).then_inc(so["ov_sel"], 1)
                                    dve.wait_ge(so["ov_wt"], 3)
                                    dve.wait_ge(so["ov_sel"], 1)
                                    v.tensor_tensor(selm[1], selm[0], r1[2].unsqueeze(2).to_broadcast([P, NT, CAP]),
                                                    ALU.mult).then_inc(so["ov_selw"], 1)
                                    dve.wait_ge(so["ov_gathered"], 1)
                                    take_x(0, 2).then_inc(so["ov_xe"], 1)
                                    dve.wait_ge(so["ov_silu"], 1)
                                    v.tensor_tensor(hid[0:CAP], ps[64:P, 0, :], silu[0:CAP], ALU.mult).then_inc(so["ov_hid"], 1)
                                    for n in range(2 * NT):
                                        dve.wait_ge(so["ov_back"], n + 1)
                                        xs = x[:, n // 2, (n % 2) * 512:(n % 2 + 1) * 512]
                                        v.tensor_tensor(xs, xs, ps[:, n, :], ALU.add).then_inc(so["ov_added"], 1)
                                    dve.wait_ge(so["ov_added"], 2 * NT)

                                @block.gpsimd
                                def _(pool):
                                    g = nc.gpsimd
                                    for k in range(2):
                                        ohe = oh[k][:, :, bass.ds(e, 1)].rearrange("p t e -> p (t e)")
                                        g.tensor_tensor(r1[k], ohe, cw[k], ALU.mult).then_inc(so["ov_wt"], 1)
                                    pool.wait_ge(so["ov_wt"], 2)
                                    g.tensor_tensor(r1[2], r1[0], r1[1], ALU.add).then_inc(so["ov_wt"], 1)
                            clear(nc, over_sems)
                        with nc.Else():
                            nc.sync.sem_clear(so["ov_shift"])
                    nc.all_engine_barrier()

            with nc.Block() as block:
                @block.gpsimd
                def _(pool):
                    for k in range(2):
                        for t in range(NT):
                            nc.gpsimd.indirect_dma_start(
                                out=yg[k][t], out_offset=None, in_=io["ybuf"][:, :],
                                in_offset=bass.IndirectOffsetOnAxis(ap=didx[k][:, t:t + 1], axis=0)).then_inc(s["yg_in"], 16)

                @block.vector
                def _(dve):
                    dve.wait_ge(s["yg_in"], layer * (16 * 2 * NT) + 16 * 2 * NT)
                    n = 0
                    for k in range(2):
                        for t in range(NT):
                            if k == 1:
                                dve.wait_ge(s["comb_done"], t + 1)
                            nc.vector.scalar_tensor_tensor(x[:, t, :], yg[k][t], cwm[k][:, t:t + 1], x[:, t, :],
                                                           ALU.mult, ALU.add).then_inc(s["comb_done"], 1)
                            n += 1
                    dve.wait_ge(s["comb_done"], n)
            clear(nc, layer_sems)

        fin = {n: sem(n) for n in ("f_in", "f_sq", "f_var", "f_sd", "f_done", "f_out", "f_chain")}
        gfin = view(O_HT, D)
        with nc.Block() as block:
            @block.sync
            def _(sp):
                sp.dma_start(gfin, io["gfin"].to_broadcast([P, D])).then_inc(fin["f_in"], 16)
                for t in range(NT):
                    sp.wait_ge(fin["f_done"], t + 1)
                    sp.dma_start(io["out"][0, t * P:(t + 1) * P, :], xn[:, t, :]).then_inc(fin["f_out"], 16)
                sp.wait_ge(fin["f_out"], 16 * NT)

            @block.scalar
            def _(act):
                for t in range(NT):
                    nc.scalar.activation(xn[:, t, :], x[:, t, :], ACT.Square, accum_out=sumsq[:, t:t + 1]).then_inc(fin["f_sq"], 1)
                act.wait_ge(fin["f_var"], 1)
                nc.scalar.activation(rstd, sumsq, ACT.Sqrt).then_inc(fin["f_sd"], 1)

            @block.vector
            def _(dve):
                dve.wait_ge(fin["f_sq"], NT)
                nc.vector.tensor_scalar(sumsq, sumsq, 1.0 / D, EPS, ALU.mult, ALU.add).then_inc(fin["f_var"], 1)
                dve.wait_ge(fin["f_sd"], 1)
                nc.vector.reciprocal(rstd, rstd).then_inc(fin["f_chain"], 1)
                dve.wait_ge(fin["f_chain"], 1)
                dve.wait_ge(fin["f_in"], 16)
                for t in range(NT):
                    nc.vector.scalar_tensor_tensor(xn[:, t, :], x[:, t, :], rstd[:, t:t + 1], gfin, ALU.mult, ALU.mult)\
                      .then_inc(fin["f_done"], 1)


N_REDUCE = 8


def reduce_angle(nc, link, ang, kk, rr, r2):
    v = nc.vector
    link(v.tensor_scalar(kk, ang, 1.0 / TWO_PI, MAGIC, ALU.mult, ALU.add))
    link(v.tensor_scalar(kk, kk, MAGIC, None, ALU.subtract))
    link(v.scalar_tensor_tensor(rr, kk, -PI_1, ang, ALU.mult, ALU.add))
    link(v.scalar_tensor_tensor(rr, kk, -PI_2, rr, ALU.mult, ALU.add))
    link(v.scalar_tensor_tensor(rr, kk, -PI_3, rr, ALU.mult, ALU.add))
    link(v.tensor_scalar(rr, rr, PI_SAFE, -PI_SAFE, ALU.min, ALU.max))
    link(v.scalar_tensor_tensor(r2, rr, -1.0, rr, ALU.mult, ALU.max))
    link(v.tensor_scalar(r2, r2, -1.0, float(np.pi / 2), ALU.mult, ALU.add))


def load_expert(nc, sp, io, expert_rows, e, b, w_gate, w_up, w_down, w_sem):
    sp.dma_start(w_gate[b], expert_rows(io["expert_w_gate"], e, ND)).then_inc(w_sem[b][0], 16)
    sp.dma_start(w_up[b], expert_rows(io["expert_w_up"], e, ND)).then_inc(w_sem[b][1], 16)
    sp.dma_start(w_down[b], expert_rows(io["expert_w_down"], e, NH)).then_inc(w_sem[b][2], 16)


def expert_gather(nc, ps, bank, xn, sel):
    for d in range(ND):
        for t in range(NT):
            last = nc.tensor.matmul(ps[:, bank, d * CAP:(d + 1) * CAP], xn[:, t, d * P:(d + 1) * P], sel[:, t, :],
                                    start=(t == 0), stop=(t == NT - 1))
    return last


def expert_gate_up(nc, ps, bank, xe, wg, wu):
    for k in range(ND):
        nc.tensor.matmul(ps[0:64, bank, :], xe[:, k, :], wg[:, k, :], start=(k == 0), stop=(k == ND - 1), tile_position=(0, 0))
        last = nc.tensor.matmul(ps[64:P, bank, :], xe[:, k, :], wu[:, k, :], start=(k == 0), stop=(k == ND - 1),
                                tile_position=(0, 64))
    return last


def expert_transpose(nc, ps, hid, ident):
    for c in range(NH):
        last = nc.tensor.matmul(ps[:, 4, c * CAP:(c + 1) * CAP], hid[0:64, c * P:(c + 1) * P], ident[0:64, 0:64], start=True, stop=True)
    return last


def expert_down(nc, ps, bank, hT, wd):
    for k in range(NH):
        for half in range(2):
            last = nc.tensor.matmul(ps[64 * half:64 * half + 64, bank, :], hT[:, k, :], wd[:, k, half * 512:(half + 1) * 512],
                                    start=(k == 0), stop=(k == NH - 1), tile_position=(0, 64 * half))
    return last


def clear(nc, sems):
    nc.all_engine_barrier()
    for x in sems:
        nc.sync.sem_clear(x)
    nc.all_engine_barrier()


def _blocks(a):
    l = a.shape[0]
    return a.reshape((l, 8, 2, 64) + a.shape[3:]).transpose((0, 2, 3, 1) + tuple(range(4, a.ndim + 1))).reshape((l, P, 8) + a.shape[3:])


def _pair_diagonal(a):
    out = np.zeros(a.shape[:3] + (2, 16), a.dtype)
    out[:, 0:64, :, 0] = a[:, 0:64]
    out[:, 64:128, :, 1] = a[:, 64:128]
    return out.reshape(a.shape[:3] + (32,))


def _chunks(a):
    l, r, n = a.shape
    return a.reshape(l, r // P, P, n).transpose(0, 2, 1, 3)


def _flat(*parts):
    return np.ascontiguousarray(np.concatenate([p.reshape(p.shape[0], P, -1) for p in parts], axis=2))


def _constants():
    c = np.zeros((P, N_CONST), np.float32)
    c[:, C_IDENT:C_IDENT + P] = np.eye(P)
    r = np.zeros((P, P), np.float32)
    for h in (0, 64):
        for m in range(HALF_ROPE):
            r[h + m + HALF_ROPE, h + m] = -1.0
            r[h + m, h + m + HALF_ROPE] = 1.0
    c[:, C_ROT:C_ROT + P] = r
    q = np.arange(P)
    c[:, C_CAUSAL:C_CAUSAL + P] = np.where(q[None, :] <= q[:, None], 0.0, NEG)
    t = (np.arange(NT)[None, :, None] * P + q[:, None, None])
    ends = np.arange(32)[None, None, :] * 16 + 31
    ok = (ends <= t) & (np.arange(32)[None, None, :] < NCMP)
    c[:, C_CADD:C_CADD + P] = np.where(ok, 0.0, NEG).reshape(P, P)
    c[:, C_C01:C_C01 + P] = ok.reshape(P, P)
    inv = (np.float32(500000.0) ** (-np.arange(HALF_ROPE, dtype=np.float32) / HALF_ROPE)).astype(np.float32)
    dim = np.arange(P) % DH
    c[:, C_FREQ] = np.where(dim < 2 * HALF_ROPE, inv[dim % HALF_ROPE], 0.0)
    m = np.zeros((P, N_MCONST), np.float32)
    m[:, M_TRI:M_TRI + P] = q[:, None] < q[None, :]
    m[:, M_ONES:M_ONES + P] = 1.0
    m[:, M_IOTA:M_IOTA + CAP] = np.arange(CAP)
    m[:, M_DESC32:M_DESC32 + 32] = 32 - np.arange(32)
    m[:, M_BASE:M_BASE + 32] = np.arange(32) * CAP
    m[:, M_DESC4:M_DESC4 + 4] = 4 - np.arange(4)
    return c, m


def _layout(i):
    a = {k: np.asarray(v) for k, v in i.items()}
    w = _chunks(a["w_in"])
    q = w[..., 0:512].reshape(L, P, ND, G, R, DH).transpose(0, 1, 2, 4, 3, 5).reshape(L, P, ND, 512)
    kc, vc, ks, vs, kw, vw = (w[..., 512 + P * n:512 + P * (n + 1)] for n in range(6))
    nsa, sgu, s5, br = w[..., 1280:1304], w[..., 1304:1816], w[..., 1816:2072], w[..., 2072:5144]

    def two(x):
        y = x.reshape(L, 32, DH, P).transpose(0, 2, 1, 3)
        return np.concatenate([y, y], axis=1)
    slabs = [sgu, np.concatenate([s5, kc, vc], 3), np.concatenate([ks, kw, q[..., 0:256]], 3),
             np.concatenate([q[..., 256:512], vs, vw], 3), two(a["cmp_k_w1"]), two(a["cmp_v_w1"])]
    slabs += [br[..., n * 512:(n + 1) * 512] for n in range(6)]
    slabs += [_chunks(a["w_attn_o"]), np.concatenate([_chunks(a["w_sgu_o"]), _chunks(a["w_s5_o"])], 2)]
    mix = _chunks(a["w_mix_o"])
    slabs += [mix[..., 0:512], mix[..., 512:1024]]
    dense = np.stack([x.reshape(L, P, SLAB) for x in slabs], axis=1)

    def cols(x, n):
        return x.reshape(L, n, P).transpose(0, 2, 1)

    pos = [np.concatenate([a[k].transpose(0, 2, 1), np.zeros((L, DH, 32), np.float32)], 1) for k in ("cmp_pos_k", "cmp_pos_v")]
    w2k = a["cmp_k_w2"]
    step = np.repeat(a["s5_log_step"][:, :, None], 64, axis=2)
    small = _flat(cols(a["norm_mix_g"], 8), cols(a["norm_ffn_g"], 8), _blocks(a["s5_a_re"]), _blocks(a["s5_a_im"]), _blocks(step),
                  cols(a["s5_d"], 2), cols(a["s5_glu_b"], 2), a["sgu_b"].transpose(0, 2, 1), a["cmp_v_w2"],
                  np.concatenate([w2k, w2k], 2), pos[0], pos[1], nsa)
    bparam = _flat(_pair_diagonal(_blocks(a["s5_b_re"])), _pair_diagonal(_blocks(a["s5_b_im"])))
    cc = [_pair_diagonal(_blocks(a[k].transpose(0, 1, 3, 2))) for k in ("s5_c_re", "s5_c_im")]
    cglu = _flat(cc[0], cc[1], _chunks(a["s5_glu_w"]))
    sgup = _flat(a["sgu_w"].transpose(0, 3, 1, 2), np.repeat(a["sgu_norm_g"][:, None, :], P, axis=1))
    rb = np.concatenate([a["router_group_b"], a["router_expert_b"]], 1)
    router = _flat(_chunks(np.concatenate([a["router_group_w"], a["router_expert_w"]], 2)), np.repeat(rb[:, None, :], P, axis=1))
    consts, mconsts = _constants()
    return dict(x=a["x"], positions=a["positions"], dense=dense, small=small, bparam=bparam, cglu=cglu, sgup=sgup, router=router,
                consts=consts, mconsts=mconsts, gfin=a["norm_final_g"][None, :], expert_w_gate=a["expert_w_gate"],
                expert_w_up=a["expert_w_up"], expert_w_down=a["expert_w_down"])


def kernel(**inputs):
    import concourse.bacc as _bacc
    from concourse.bass_utils import run_bass_kernel_spmd as _run

    nc = _bacc.Bacc("TRN2", target_bir_lowering=False, num_devices=1)
    arrays = {f"in_{k}": np.ascontiguousarray(v) for k, v in _layout(inputs).items()}
    io = {k[3:]: nc.dram_tensor(k, v.shape, mybir.dt.from_np(v.dtype), kind="ExternalInput").ap() for k, v in arrays.items()}
    io["out"] = nc.dram_tensor("out_0", (1, S, D), F32, kind="ExternalOutput").ap()
    io["ybuf"] = nc.dram_tensor("expert_rows", (N_EXP * CAP, D), F32, kind="Internal").ap()
    build(nc, io)
    r = _run(nc, [arrays], core_ids=[0])
    return r.results[0]["out_0"]
```

```python
from contextlib import ExitStack

import numpy as np

import concourse.bass as bass
from concourse import mybir

F32 = mybir.dt.float32
I32 = mybir.dt.int32
F32R = mybir.dt.float32r
ALU = mybir.AluOpType
ACT = mybir.ActivationFunctionType
AX = mybir.AxisListType.X

P = 128
D = 1024
S = 512
L = 2
NT = S // P
ND = D // P
H, G, R, DH = 8, 2, 4, 64
NCMP = 31
HALF_ROPE = 8
N_EXP, N_GRP, E_PER = 32, 4, 8
HID = 512
NH = HID // P
CAP = 64
SG = 4
NCH = 8
EPS = 1e-6
NEG = -1.0e30
MAGIC = 12582912.0
TWO_PI = 2.0 * np.pi
PI_1 = 6.28125
PI_2 = float(np.float32(np.round((TWO_PI - PI_1) * 2.0**19) / 2.0**19))
PI_3 = float(np.float32(TWO_PI - PI_1 - PI_2))
PI_SAFE = 3.1415925

SMALL = dict(gmix=(0, 8), gffn=(8, 8), a_re=(16, 8), a_im=(24, 8), lstep=(32, 8), d=(40, 2), glub=(42, 2),
             sgub=(44, 4), w2v=(48, 64), w2k=(112, 128), posk=(240, 32), posv=(272, 32), wnsa=(304, 192))
N_SMALL = 496
C_IDENT, C_ROT, C_CAUSAL, C_CADD, C_C01, C_FREQ = 0, 128, 256, 384, 512, 640
N_CONST = 641
M_TRI, M_ONES, M_IOTA, M_DESC32, M_BASE, M_DESC4 = 0, 128, 256, 320, 352, 384
N_MCONST = 388

O_X = 0
O_XN = 4096
O_HT = 8192
O_SLAB = 12288
O_GATE = 24576
O_KS = 36864
O_KW = 37888
O_KC = 38912
O_V = 41984
O_Z = 43104
O_OACC = 45152
O_YST = 47200
O_XS = 48224
O_S5 = 49248
N_BRANCH = 3072
O_CONST = 50272
O_ROPE = O_CONST + N_CONST
O_SMALL = O_ROPE + 1024
O_BBT = O_SMALL + N_SMALL
O_STAT = O_BBT + 512
N_STAT = 192
O_END = O_STAT + N_STAT
assert O_YST + N_BRANCH == O_CONST and O_END <= 53215

SLAB = 4096
N_SLAB = 15
S_GATE, S_ATT, S_SGU, S_MIX = 5, 11, 12, 13
J_HT, J_SGU, J_S5, J_KC, J_KS, J_Q, J_V, J_GATE, J_MIX, J_H2 = 0, 8, 12, 14, 16, 18, 22, 26, 50, 58
J_END = 66
TAIL = [("mix", 0, 1), ("mix", 1, 1), ("h", 0, 0), ("h", 0, 1), ("mix", 2, 1), ("h", 1, 0), ("h", 1, 1), ("mix", 3, 1),
        ("h", 2, 0), ("h", 2, 1), ("h", 3, 0), ("h", 3, 1)]
J_TAIL = J_MIX + NT
assert J_TAIL + len(TAIL) == J_END
N_ATT = 2 * NT * H
CRED = 2


def build(nc, io):
    ctx = ExitStack()
    with ctx:
        def sem(name):
            return ctx.enter_context(nc.semaphore(name))

        arena = ctx.enter_context(nc.sbuf_tensor("arena", [P, O_END - N_BRANCH], F32))
        with nc.sbuf_tensor("branch", [P, N_BRANCH], F32) as branch:
            pass
        split = ctx.enter_context(nc.sbuf_tensor("split_rows", [P, N_BRANCH], F32R))
        ps = ctx.enter_context(nc.psum_tensor("ps", [P, 8, 512], F32))

        def view(off, *dims):
            n = int(np.prod(dims))
            if O_YST <= off < O_CONST:
                a = branch[:, off - O_YST:off - O_YST + n]
            elif off >= O_CONST:
                a = arena[:, off - N_BRANCH:off - N_BRANCH + n]
            else:
                a = arena[:, off:off + n]
            if len(dims) == 1:
                return a
            names = "abcd"[:len(dims)]
            return a.rearrange("p (" + " ".join(names) + ") -> p " + " ".join(names),
                               **{k: v for k, v in zip(names[1:], dims[1:])})

        x = view(O_X, NT, D)
        xn = view(O_XN, NT, D)
        q_plain = view(O_XN, 4, S)
        q_rot = view(O_XN + 2048, 4, S)
        hT = view(O_HT, ND, S)
        slab = [O_SLAB + i * SLAB for i in range(3)]
        tab_re = view(O_GATE, NCH, S)
        tab_im = view(O_GATE + 4096, NCH, S)
        tab_tmp = O_GATE + 8192
        sgu_w = view(O_GATE + 10240, SG, P)
        sgu_g = view(O_GATE + 10752, 256)
        s5_c = view(O_GATE + 10240, S)
        s5_d = view(O_GATE + 10752, S)
        s5_ab = [[view(O_Z + (2 * b + i) * S, S) for i in range(2)] for b in range(2)]
        gates = view(O_GATE, 24, S)
        k_sel = view(O_KS, 2, S)
        k_win = view(O_KW, 2, S)
        c_in = [view(O_KC, 3, S), view(O_KC + 1536, 3, S)]
        oT = view(O_KC, 4, S)
        O_CW = O_KC + 2048
        v_cmp = view(O_CW, G, R * DH)
        k_cmp = view(O_CW + 512, G, 32)
        k_hid = view(O_CW + 576, G, 32)
        v_hid = view(O_CW + 640, G, R, 32)
        c_bias = view(O_CW + 896, 2)
        c_max = view(O_CW + 898, 32)
        c_sum = view(O_CW + 930, 32)
        o_tmp = view(O_CW, S)
        v_tok = view(O_V, NT, 256)
        nsa_g = view(O_V + 1024, NT, 24)
        z = view(O_Z, NT, S)
        prob = [view(O_Z + i * S, S) for i in range(2)]
        probT = [view(O_Z + 1024 + i * S, S) for i in range(2)]
        c_sc = view(O_Z, NT, H, 32)
        c_scf = view(O_Z, NT * H, 32)
        m_tmp = [view(O_Z + i * S, S) for i in range(2)]
        vn = view(O_OACC, NT, 256)
        ys = view(O_OACC + 1024, NT, 256)
        cc = view(O_OACC, 2, NCH, 32)
        glu_w = view(O_OACC + 512, 2, 256)
        oacc = view(O_OACC, NT, S)
        ysT = view(O_YST, 2, S)
        b_in = view(O_YST, 2, NCH, 32)
        s5_small = [view(O_YST + 512 + 8 * i, 8) for i in range(16)]
        xsT = view(O_XS, 2, S)
        s5T = view(O_S5, 2, S)
        bbar = view(O_S5, 2, NCH, 32)
        bb_tmp = view(O_S5 + 512, NCH, 32)
        cst = view(O_CONST, N_CONST)
        ident = cst[:, C_IDENT:C_IDENT + P]
        rot = cst[:, C_ROT:C_ROT + P]
        causal = cst[:, C_CAUSAL:C_CAUSAL + P]
        c_add = view(O_CONST + C_CADD, NT, 32)
        c_01 = view(O_CONST + C_C01, NT, 32)
        freq = cst[:, C_FREQ:C_FREQ + 1]
        rope_cos = view(O_ROPE, S)
        rope_sin = view(O_ROPE + S, S)
        small = {k: view(O_SMALL + a, n) for k, (a, n) in SMALL.items()}
        wnsa = view(O_SMALL + SMALL["wnsa"][0], ND, 24)
        bbT = view(O_BBT, 2, 2, P)
        st = O_STAT
        mag = view(st, 8)
        cos1 = view(st + 8, 8)
        sin1 = view(st + 16, 8)
        pw = [view(st + 24 + 8 * i, 8) for i in range(4)]
        sumsq = view(st + 56, 4)
        rstd = view(st + 60, 4)
        vsumsq = view(st + 64, 4)
        vrstd = view(st + 68, 4)
        rowmax = view(st + 72, 4)
        rowsum = view(st + 76, N_ATT)
        rinv = view(st + 140, 8)
        wgt = view(st + 148, 8)
        glub_h = view(st + 156, 2)
        sincos = [view(st + 160 + 8 * i, 8) for i in range(4)]

        A = O_KS
        mc = view(A, N_MCONST)
        tri = mc[:, M_TRI:M_TRI + P]
        ones = mc[:, M_ONES:M_ONES + P]
        iota = mc[:, M_IOTA:M_IOTA + CAP]
        desc32 = mc[:, M_DESC32:M_DESC32 + 32]
        base_e = mc[:, M_BASE:M_BASE + 32]
        desc4 = mc[:, M_DESC4:M_DESC4 + 4]
        A += N_MCONST
        rw = view(A, ND, 36)
        rb = view(A + 288, 36)
        A += 324
        logit = view(A, NT, 36); A += 144
        logitT = view(A, S); A += 512
        gtmp = view(A, NT, 4); A += 16
        goh = view(A, NT, 4); A += 16
        em = view(A, NT, 32); A += 128
        eq = view(A, NT, 32); A += 128
        oh = [view(A + 128 * i, NT, 32) for i in range(2)]; A += 256
        sel_all = view(A, NT, 32); A += 128
        before = view(A, NT, 32); A += 128
        slot = view(A, N_EXP + 2, NT); A += 136
        r1 = [view(A + 4 * i, NT) for i in range(10)]; A += 40
        cw = [view(A + 4 * i, NT) for i in range(2)]; A += 8
        wtab = view(A, N_EXP, NT); A += 128
        countf = view(A, N_EXP + 1); A += 34
        counts = view(A, N_EXP + 1).bitcast(I32); A += 34
        sel = view(A, NT, 2 * CAP)
        ov_sel = [view(A + 256 * i, NT, CAP) for i in range(2)]; A += 512
        ov_xe = view(A, ND, CAP)
        xe = [view(A + 1024 * i, ND, 2 * CAP) for i in range(2)]; A += 2048
        silu = view(A, HID); A += 512
        hid = view(A, HID); A += 512
        hidT = [view(A + 256 * i, NH, CAP) for i in range(2)]; A += 512
        selw = view(A, NT, 2 * CAP); A += 512
        selT = split[:, 0:S]
        y_hi = split[:, S:S + D]
        y_lo = split[:, S + D:S + 2 * D]
        w_slot = view(A, 1); A += 2
        table_in = view(A, 1); A += 2
        ov_selT = silu
        ov_y = view(A, D); A += 1024
        assert A <= O_YST
        wslot = [[O_GATE + i * SLAB for i in range(3)], [O_SLAB + i * SLAB for i in range(3)]]
        w_gate = [view(w[0], ND, HID) for w in wslot]
        w_up = [view(w[1], ND, HID) for w in wslot]
        w_down = [view(w[2], NH, D) for w in wslot]

        def gf(n):
            return small["gffn"].unsqueeze(2).to_broadcast([P, ND, n])

        def build_pair(i):
            return nc.vector.tensor_tensor(sel.rearrange("p t (b c) -> p t b c", b=2),
                                           iota.unsqueeze(1).unsqueeze(1).to_broadcast([P, NT, 2, CAP]),
                                           slot[:, bass.ds(2 * i, 2), :].rearrange("p e t -> p t e").unsqueeze(3)
                                           .to_broadcast([P, NT, 2, CAP]), ALU.is_equal)

        BANK_BACK = [5, 7]
        BANK_P, BANK_S, BANK_T, BANK_O = [0, 1], [2, 3], [4, 5], [6, 7]

        s = {n: sem(n) for n in ("pro_in", "pro_dve", "pro_act")}
        pos_i = view(O_XN, S).bitcast(I32)
        ang, kk, rr, r2 = (view(O_XN + 512 * i, S) for i in range(1, 5))
        with nc.Block() as block:
            @block.sync
            def _(sp):
                sp.dma_start(x, io["x"].rearrange("b (t p) d -> p (b t) d", p=P)).then_inc(s["pro_in"], 16)
                sp.dma_start(cst, io["consts"]).then_inc(s["pro_in"], 16)
                sp.dma_start(pos_i, io["positions"].to_broadcast([P, S])).then_inc(s["pro_in"], 16)

            @block.vector
            def _(dve):
                dve.wait_ge(s["pro_in"], 48)
                n = 0

                def link(ins):
                    nonlocal n
                    ins.then_inc(s["pro_dve"], 1)
                    n += 1
                    dve.wait_ge(s["pro_dve"], n)
                link(nc.vector.tensor_copy(rr, pos_i))
                link(nc.vector.tensor_scalar(ang, rr, freq, None, ALU.mult))
                reduce_angle(nc, link, ang, kk, rr, r2)

            @block.scalar
            def _(act):
                act.wait_ge(s["pro_dve"], 2 + N_REDUCE)
                nc.scalar.activation(rope_sin, rr, ACT.Sin).then_inc(s["pro_act"], 1)
                nc.scalar.activation(rope_cos, r2, ACT.Sin).then_inc(s["pro_act"], 1)
                act.wait_ge(s["pro_act"], 2)

        names = ("small_in", "bparam_in", "sgu_in", "cglu_in", "router_in", "mconst_in", "slab_in0", "slab_in1", "slab_in2",
                 "chain_dve", "chain_act", "chain_pool", "sumsq_ready", "var_ready", "sd_ready", "xn_ready",
                 "step_ready", "lam_ready", "mag_ready", "angle_ready", "sincos_ready", 
                 "planes_clear", "bb_ready", "bb_done", "bb_evac", "proj_done", "proj_free",
                 "vsq_ready", "vvar_ready", "vsd_ready", "vn_ready", "sgu_w_ready", "mixed_done", "mixed_evac", "ysT_done", "ysT_evac",
                 "bu_done", "twist_read", "h_ready", "y_done", "rot_done", "rope_done", "y1_ready", "gelu_done",
                 "glu_done", "glu_read", "s5_done", "hidden_done", "hid_ready", "ckv_done", "ckv_ready", "cs_done", "cs_read",
                 "cexp_in", "cexp_done", "cp_ready", "ct_done", "ct_evac", "oc_done", "oc_evac",
                 "scores_done", "max_done", "exp_done", "tr_done", "pt_evac", "pv_done", "o_evac",
                 "oT_done", "oT_evac", "outp_done", "merge_done", "nsa_tanh", "nsa_ready",
                 "rt_done", "rt_read", "gexp_in", "gexp_done", "e2_in", "e2_done", "sel_ready", "rank_done", "route_done",
                 "x_gathered", "sel_built", "xe_ready", "gu_done", "silu_done", "hid_done", "hT_done", "hT_read",
                 "down_done", "y_read", "y_lo_ready", "pair_zero", "selw_ready", "slot_weight", "table_in", "selT_done", "selT_read", "back_done", "back_added",
                 "we0g", "we0u", "we0d", "we1g", "we1u", "we1d")
        s.update({n: sem(n) for n in names})
        slab_in = [s["slab_in0"], s["slab_in1"], s["slab_in2"]]
        w_in_sem = [[s["we0g"], s["we0u"], s["we0d"]], [s["we1g"], s["we1u"], s["we1d"]]]
        over_names = ("ov_shift", "ov_weights", "ov_sel", "ov_gathered", "ov_xe", "ov_gu", "ov_selw", "ov_selT",
                      "ov_silu", "ov_hid", "ov_hT", "ov_hT_read", "ov_selT_read", "ov_down", "ov_y", "ov_back", "ov_added")
        so = {n: sem(n) for n in over_names}
        over_sems = list(so.values())
        layer_sems = [s[n] for n in names]

        with nc.Fori(0, L) as layer:
            def row(ap):
                return ap[bass.ds(layer, 1)].rearrange("l p n -> (l p) n")

            def expert_rows(ap, e, k):
                return ap[bass.ds(layer, 1), bass.ds(e, 1)].rearrange("l e (k p) n -> p (l e k) n", p=P, k=k)

            with nc.Block() as block:
                @block.sync
                def _(sp):
                    sp.dma_start(view(O_SMALL, N_SMALL), row(io["small"])).then_inc(s["small_in"], 16)
                    sp.dma_start(view(O_YST, 512), row(io["bparam"])).then_inc(s["bparam_in"], 16)
                    sp.dma_start(view(O_GATE + 10240, 768), row(io["sgup"])).then_inc(s["sgu_in"], 16)
                    free = {3: (s["proj_done"], J_S5), 4: (s["proj_done"], J_KS), 5: (s["proj_done"], J_KS + 4),
                            6: (s["proj_done"], J_GATE), 7: (s["hidden_done"], 2), 14: (s["outp_done"], ND)}
                    for k in range(8, 14):
                        free[k] = (s["proj_done"], J_GATE + 4 * (k - 8) + 4)
                    for k in range(N_SLAB):
                        if k in free:
                            sp.wait_ge(*free[k])
                        if k == 4:
                            sp.wait_ge(s["ysT_done"], 2)
                            sp.dma_start(view(O_OACC, 1024), row(io["cglu"])).then_inc(s["cglu_in"], 16)
                        src = io["dense"][bass.ds(layer, 1), k].rearrange("l p n -> (l p) n")
                        sp.dma_start(view(slab[k % 3], SLAB), src).then_inc(slab_in[k % 3], 16)
                    sp.wait_ge(s["merge_done"], ND)
                    load_expert(nc, sp, io, expert_rows, 0, 0, w_gate, w_up, w_down, w_in_sem)
                    sp.wait_ge(s["outp_done"], ND)
                    sp.dma_start(view(O_KS + N_MCONST, 324), row(io["router"])).then_inc(s["router_in"], 16)
                    sp.dma_start(mc, io["mconsts"]).then_inc(s["mconst_in"], 16)
                    sp.wait_ge(s["proj_done"], J_END - 4)
                    load_expert(nc, sp, io, expert_rows, 1, 1, w_gate, w_up, w_down, w_in_sem)
                    with sp.Fori(0, N_EXP // 2 - 1) as i:
                        for b in range(2):
                            e = 2 * i + 2 + b
                            sp.wait_ge(s["gu_done"], 2 * i + b + 1 + CRED)
                            sp.dma_start(w_gate[b], expert_rows(io["expert_w_gate"], e, ND)).then_inc(w_in_sem[b][0], 16)
                            sp.dma_start(w_up[b], expert_rows(io["expert_w_up"], e, ND)).then_inc(w_in_sem[b][1], 16)
                            sp.wait_ge(s["down_done"], 2 * i + b + 1 + CRED)
                            sp.dma_start(w_down[b], expert_rows(io["expert_w_down"], e, NH)).then_inc(w_in_sem[b][2], 16)

                @block.tensor
                def _(pe):
                    def wait_slab(k):
                        pe.wait_ge(slab_in[k % 3], 16 * (k // 3 + 1))

                    def bank_p(n):
                        if n >= 2:
                            pe.wait_ge(s["proj_free"], n - 1)
                        return ps[:, BANK_P[n % 2], :]

                    def feature_job(n, w, col):
                        out = bank_p(n)
                        for k in range(ND):
                            last = nc.tensor.matmul(out, w[:, k, col:col + P], hT[:, k, :], start=(k == 0), stop=(k == ND - 1))
                        last.then_inc(s["proj_done"], 1)

                    def token_job(n, w, lo, hi, t):
                        out = bank_p(n)
                        for k in range(ND):
                            last = nc.tensor.matmul(out[:, 0:hi - lo], hT[:, k, t * P:(t + 1) * P], w[:, k, lo:hi],
                                                    start=(k == 0), stop=(k == ND - 1))
                        last.then_inc(s["proj_done"], 1)

                    def value_job(t):
                        out = bank_p(J_V + t)
                        for k in range(ND):
                            nc.tensor.matmul(out[:, 0:256], hT[:, k, t * P:(t + 1) * P], W[0][:, k, 256:S], start=(k == 0), stop=(k == ND - 1))
                        for k in range(ND):
                            last = nc.tensor.matmul(out[:, 256:280], hT[:, k, t * P:(t + 1) * P], wnsa[:, k, :],
                                                    start=(k == 0), stop=(k == ND - 1))
                        last.then_inc(s["proj_done"], 1)

                    def transpose_x(n, t, half):
                        out = bank_p(n)
                        for d in range(4):
                            f = (4 * half + d) * P
                            last = nc.tensor.transpose(out[:, d * P:(d + 1) * P], xn[:, t, f:f + P], ident)
                        last.then_inc(s["proj_done"], 1)

                    W = [view(slab[k % 3], ND, S) for k in range(3)]
                    for t in range(NT):
                        pe.wait_ge(s["xn_ready"], t + 1)
                        for half in range(2):
                            transpose_x(J_HT + 2 * t + half, t, half)
                    pe.wait_ge(s["proj_free"], ND)
                    wait_slab(0)
                    for t in range(NT):
                        token_job(J_SGU + t, W[0], 0, S, t)
                    pe.wait_ge(s["bb_ready"], 1)
                    for J in range(2):
                        for ri in range(2):
                            last = nc.tensor.transpose(ps[:, BANK_T[0], (2 * J + ri) * P:(2 * J + ri + 1) * P],
                                                       bbar[:, ri, 4 * J:4 * J + 4, :].rearrange("p a b -> p (a b)"), ident)
                    last.then_inc(s["bb_done"], 1)
                    wait_slab(1)
                    for c in range(2):
                        feature_job(J_S5 + c, W[1], c * P)
                    for c in range(2):
                        feature_job(J_KC + c, W[1], 256 + c * P)
                    def s5_input(j):
                        J, r = j // 4, 32 * (j % 4)
                        if j == 0:
                            pe.wait_ge(s["proj_free"], J_S5 + 2)
                        else:
                            pe.wait_ge(s["twist_read"], j)
                        for ri in range(2):
                            last = nc.tensor.matmul(ps[:, BANK_S[ri], :], bbT[r:r + 32, J, ri, :], xsT[r:r + 32, J, :],
                                                    start=True, stop=True, tile_position=(r, 0))
                        last.then_inc(s["bu_done"], 1)

                    pe.wait_ge(s["vn_ready"], NT)
                    pe.wait_ge(s["sgu_w_ready"], 1)
                    for g in range(SG):
                        last = nc.tensor.matmul(ps[:, BANK_S[g // 2], (g % 2) * 256:(g % 2 + 1) * 256], sgu_w[:, g, :],
                                                vn[:, :, g * 64:(g + 1) * 64], start=True, stop=True)
                        last.then_inc(s["mixed_done"], 1)
                    pe.wait_ge(s["mixed_evac"], SG)
                    pe.wait_ge(s["bb_evac"], 1)
                    s5_input(0)
                    wait_slab(2)
                    feature_job(J_KS, W[2], 0)
                    for c in range(2):
                        for t in range(NT):
                            last = nc.tensor.transpose(ps[:, BANK_T[c], t * P:(t + 1) * P], ys[:, t, c * P:(c + 1) * P], ident)
                        last.then_inc(s["ysT_done"], 1)

                    def s5_output(j):
                        J, r = j // 4, 32 * (j % 4)
                        if j == 0:
                            pe.wait_ge(s["cglu_in"], 16)
                        pe.wait_ge(s["h_ready"], j + 1)
                        for ri in range(2):
                            last = nc.tensor.matmul(ps[r:r + 32, BANK_O[J], :], cc[:, ri, j, :], s5_ab[j % 2][ri],
                                                    start=(ri == 0), stop=(ri == 1), tile_position=(0, r))
                        last.then_inc(s["y_done"], 1)

                    def rotate(n):
                        pe.wait_ge(s["proj_free"], J_KS + n + 1)
                        if n < 2:
                            pe.wait_ge(s["ysT_evac"], 2)
                        else:
                            pe.wait_ge(s["rope_done"], n - 1)
                        raw = q_rot[:, n, :] if n < 2 else q_plain[:, n - 2, :]
                        nc.tensor.matmul(ps[:, BANK_T[n % 2], :], rot, raw, start=True, stop=True).then_inc(s["rot_done"], 1)

                    def hidden(i):
                        wait_slab(4)
                        w = view(slab[1] + 2048 * i, 16, P)
                        pe.wait_ge(s["rope_done"], 5 + i)
                        for l in range(0, 32, 2):
                            last = nc.tensor.matmul(ps[:, BANK_T[i], 0:93].rearrange("p (a b) -> p a b", a=3), w[:, l // 2, :],
                                                    c_in[i][:, :, l:l + 16 * 30 + 1:16], start=(l == 0), stop=(l == 30))
                        last.then_inc(s["hidden_done"], 1)

                    for u in range(10):
                        if 1 <= u < NCH:
                            s5_input(u)
                        if 1 <= u < 6:
                            if u == 4:
                                wait_slab(3)
                            feature_job(J_KS + u, W[2 if u < 4 else 0], (u % 4) * P)
                        elif u == 6:
                            for t in range(2):
                                value_job(t)
                        elif u == 7:
                            for t in range(2, NT):
                                value_job(t)
                        elif u == 8:
                            pe.wait_ge(s["planes_clear"], 4)
                            hidden(0)
                        elif u == 9:
                            hidden(1)
                        if 1 <= u <= 6:
                            rotate(u - 1)
                        if 1 <= u <= NCH:
                            s5_output(u - 1)

                    filled = [0]

                    def fill(m):
                        for _ in range(m):
                            if filled[0] >= 24 * ND:
                                return
                            n, k = divmod(filled[0], ND)
                            if k == 0:
                                if n % 4 == 0:
                                    wait_slab(S_GATE + n // 4)
                                fill.out = bank_p(J_GATE + n)
                            w = view(slab[(S_GATE + n // 4) % 3], ND, S)
                            last = nc.tensor.matmul(fill.out, w[:, k, (n % 4) * P:(n % 4 + 1) * P], hT[:, k, :],
                                                    start=(k == 0), stop=(k == ND - 1))
                            if k == ND - 1:
                                last.then_inc(s["proj_done"], 1)
                            filled[0] += 1

                    fill(4)
                    pe.wait_ge(s["gelu_done"], 2)
                    for m in range(2):
                        for k in range(2):
                            last = nc.tensor.matmul(ps[:, BANK_S[m], :], glu_w[:, k, m * P:(m + 1) * P], xsT[:, k, :],
                                                    start=(k == 0), stop=(k == 1))
                        last.then_inc(s["glu_done"], 1)
                    pe.wait_ge(s["hid_ready"], 2)
                    nc.tensor.matmul(ps[:, BANK_T[0], 0:64], small["w2k"], k_hid.rearrange("p a b -> p (a b)"),
                                     start=True, stop=True)
                    for g in range(G):
                        last = nc.tensor.matmul(ps[:, BANK_T[1], g * 64:(g + 1) * 64],
                                                v_hid[:, g].rearrange("p a b -> p (a b)"), small["w2v"],
                                                start=True, stop=True)
                    last.then_inc(s["ckv_done"], 1)
                    fill(8)
                    pe.wait_ge(s["ckv_ready"], 1)
                    pe.wait_ge(s["glu_read"], 2)
                    for t in range(NT):
                        for h in range(H):
                            col = (t % 2) * 256 + h * 32
                            last = nc.tensor.matmul(ps[:, BANK_S[t // 2], col:col + 32], q_plain[:, h % 4, t * P:(t + 1) * P],
                                                    k_cmp[:, h // 4, :], start=True, stop=True)
                    last.then_inc(s["cs_done"], 1)
                    fill(12)
                    pe.wait_ge(s["cp_ready"], 1)
                    for b in range(2):
                        for i in range(4):
                            t, g = 2 * b + i // 2, i % 2
                            last = nc.tensor.transpose(ps[:, BANK_T[b], i * P:(i + 1) * P],
                                                       c_sc[:, t, g * R:(g + 1) * R, :].rearrange("p a b -> p (a b)"), ident)
                        last.then_inc(s["ct_done"], 1)
                    fill(3)
                    for t in range(NT):
                        pe.wait_ge(s["ct_evac"], t // 2 + 1)
                        if t >= 2:
                            pe.wait_ge(s["oc_evac"], t - 1)
                        for g in range(G):
                            i = (t % 2) * 2 + g
                            last = nc.tensor.matmul(ps[:, BANK_O[t % 2], g * 256:(g + 1) * 256],
                                                    probT[t // 2][:, i * P:(i + 1) * P], v_cmp[:, g, :], start=True, stop=True)
                        last.then_inc(s["oc_done"], 1)

                    pe.wait_ge(s["rope_done"], 6)
                    pe.wait_ge(s["oc_evac"], NT)

                    def step_of(i):
                        return i // 32, (i // 8) % NT, i % 8

                    def scores(i):
                        br, t, h = step_of(i)
                        n = (t + 1) * P
                        if i >= 2:
                            pe.wait_ge(s["exp_done"], i - 1)
                        keys = (k_sel, k_win)[br]
                        out = ps[:, BANK_S[i % 2], 0:n]
                        nc.tensor.matmul(out, q_rot[:, h % 4, t * P:(t + 1) * P], keys[:, h // 4, 0:n], start=True, stop=False)
                        nc.tensor.matmul(out[:, t * P:n], ident, causal, start=False, stop=True).then_inc(s["scores_done"], 1)

                    def transposes(i):
                        t = step_of(i)[1]
                        pe.wait_ge(s["exp_done"], i + 1)
                        if i >= 2:
                            pe.wait_ge(s["pt_evac"], i - 1)
                        for b in range(t + 1):
                            last = nc.tensor.transpose(ps[:, BANK_T[i % 2], b * P:(b + 1) * P], prob[i % 2][:, b * P:(b + 1) * P], ident)
                        last.then_inc(s["tr_done"], 1)

                    def values(i):
                        br, t, h = step_of(i)
                        k = i // 8
                        pe.wait_ge(s["pt_evac"], i + 1)
                        if h == 0 and k >= 2:
                            pe.wait_ge(s["o_evac"], k - 1)
                        c0 = br * P + (h // 4) * DH
                        for b in range(t + 1):
                            last = nc.tensor.matmul(ps[:, BANK_O[k % 2], h * DH:(h + 1) * DH], probT[i % 2][:, b * P:(b + 1) * P],
                                                    v_tok[:, b, c0:c0 + DH], start=(b == 0), stop=(b == t))
                        last.then_inc(s["pv_done"], 1)

                    for i in range(N_ATT + 2):
                        if i < N_ATT:
                            scores(i)
                        fill(3)
                        if 1 <= i <= N_ATT:
                            transposes(i - 1)
                        if i >= 2:
                            values(i - 2)
                    fill(24 * ND)

                    pe.wait_ge(s["o_evac"], 8)
                    pe.wait_ge(s["pt_evac"], N_ATT)
                    for c in range(4):
                        if c >= 2:
                            pe.wait_ge(s["oT_evac"], c - 1)
                        for t in range(NT):
                            last = nc.tensor.transpose(ps[:, BANK_T[c % 2], t * P:(t + 1) * P], oacc[:, t, c * P:(c + 1) * P], ident)
                        last.then_inc(s["oT_done"], 1)
                    wait_slab(S_ATT)
                    wait_slab(S_SGU)
                    pe.wait_ge(s["oT_evac"], 4)
                    pe.wait_ge(s["exp_done"], N_ATT)
                    pe.wait_ge(s["s5_done"], 2)
                    wa = view(slab[S_ATT % 3], 4, D)
                    wb = view(slab[S_SGU % 3], 4, D)
                    for n in range(ND):
                        if n >= 2:
                            pe.wait_ge(s["merge_done"], n - 1)
                        for bank, w, k0, src, nk in ((BANK_S, wa, 0, oT, 4), (BANK_T, wb, 0, ysT, 2), (BANK_O, wb, 2, s5T, 2)):
                            for k in range(nk):
                                last = nc.tensor.matmul(ps[:, bank[n % 2], :], w[:, k0 + k, n * P:(n + 1) * P], src[:, k, :],
                                                        start=(k == 0), stop=(k == nk - 1))
                        last.then_inc(s["outp_done"], 1)
                    pe.wait_ge(s["merge_done"], ND)
                    wait_slab(S_MIX)
                    for t in range(NT):
                        token_job(J_MIX + t, view(slab[S_MIX % 3], ND, S), 0, S, t)
                    wait_slab(S_MIX + 1)
                    for n, (kind, t, half) in enumerate(TAIL):
                        if kind == "mix":
                            token_job(J_TAIL + n, view(slab[(S_MIX + 1) % 3], ND, S), 0, S, t)
                        else:
                            pe.wait_ge(s["xn_ready"], NT + t + 1)
                            transpose_x(J_TAIL + n, t, half)
                    pe.wait_ge(s["proj_free"], J_END)
                    pe.wait_ge(s["router_in"], 16)
                    for k in range(ND):
                        last = nc.tensor.matmul(ps[0:36, BANK_S[0], :], rw[:, k, :], hT[:, k, :], start=(k == 0), stop=(k == ND - 1))
                    last.then_inc(s["rt_done"], 1)
                    pe.wait_ge(s["rt_read"], 1)
                    for t in range(NT):
                        last = nc.tensor.matmul(ps[:, BANK_S[1], t * 36:(t + 1) * 36], logitT[:, t * P:(t + 1) * P], ident[:, 0:36],
                                                start=True, stop=True)
                    last.then_inc(s["rt_done"], 1)
                    pe.wait_ge(s["sel_ready"], 1)
                    flat = sel_all.rearrange("p t e -> p (t e)")
                    nc.tensor.matmul(ps[:, BANK_T[0], 0:P], tri, flat, start=True, stop=True)
                    last = nc.tensor.matmul(ps[:, BANK_T[1], 0:P], ones, flat, start=True, stop=True)
                    last.then_inc(s["rank_done"], 1)

                    pe.sem_inc(s["gu_done"], CRED)
                    pe.sem_inc(s["hT_done"], CRED)
                    pe.sem_inc(s["down_done"], CRED)
                    pe.sem_inc(s["selT_done"], CRED)
                    pe.wait_ge(s["sel_built"], 1)
                    pe.wait_ge(s["route_done"], 1)
                    pe.wait_ge(s["pair_zero"], 5)

                    def rows_ready(i):
                        pe.wait_ge(s["selT_read"], i + CRED)
                        pe.wait_ge(s["y_read"], 4 * i + CRED)
                        pe.wait_ge(s["y_lo_ready"], 4 * i + CRED)

                    def row_back(i, n):
                        pe.wait_ge(s["back_added"], 8 * i + n - 1 + 8)
                        to = selT[:, (n // 2) * P:(n // 2 + 1) * P]
                        out = ps[:, BANK_BACK[n % 2], :]
                        cols = slice((n % 2) * 512, (n % 2 + 1) * 512)
                        nc.tensor.matmul(out, to, y_hi[:, cols], start=True, stop=False)
                        nc.tensor.matmul(out, to, y_lo[:, cols], start=False, stop=True).then_inc(s["back_done"], 1)

                    def gather_pair():
                        for d in range(ND):
                            for t in range(NT):
                                last = nc.tensor.matmul(ps[:, 2 + d // 4, (d % 4) * P:(d % 4 + 1) * P],
                                                        xn[:, t, d * P:(d + 1) * P], sel[:, t, :], start=(t == 0), stop=(t == NT - 1))
                        last.then_inc(s["x_gathered"], 1)

                    gather_pair()
                    with pe.Fori(0, N_EXP // 4) as j:
                        for q in range(2):
                            i = 2 * j + q
                            for b in range(2):
                                e = 2 * i + b
                                if b == 0:
                                    pe.wait_ge(s["xe_ready"], i + 1)
                                pe.wait_ge(s["hid_done"], e + CRED)
                                pe.wait_ge(w_in_sem[b][0], 32 * j + 16 * q + 16)
                                pe.wait_ge(w_in_sem[b][1], 32 * j + 16 * q + 16)
                                for k in range(ND):
                                    if b == 0 and k >= 4:
                                        if k == 4:
                                            rows_ready(i)
                                        row_back(i, k - 4)
                                    last = expert_gate_up(nc, ps, 0, xe[q][:, k, 64 * b:64 * b + 64], w_gate[b][:, k, :], w_up[b][:, k, :], k)
                                last.then_inc(s["gu_done"], 1)
                                if b == 0:
                                    for n in range(4, 8):
                                        row_back(i, n)
                                    pe.wait_ge(s["selw_ready"], i + 1)
                                    for t in range(NT):
                                        last = nc.tensor.transpose(ps[:, 1, t * P:(t + 1) * P], selw[:, t, :], ident)
                                    last.then_inc(s["selT_done"], 1)
                                else:
                                    pe.wait_ge(s["sel_built"], i + 2)
                                    gather_pair()
                                pe.wait_ge(s["hid_done"], e + 1 + CRED)
                                pe.wait_ge(s["hT_read"], e + CRED)
                                expert_transpose(nc, ps, hid, ident).then_inc(s["hT_done"], 1)
                                pe.wait_ge(s["hT_read"], e + 1 + CRED)
                                pe.wait_ge(w_in_sem[b][2], 32 * j + 16 * q + 16)
                                pe.wait_ge(s["y_lo_ready"], 2 * e + CRED)
                                expert_down(nc, ps, 6, hidT[b], w_down[b]).then_inc(s["down_done"], 1)
                    rows_ready(N_EXP // 2)
                    for n in range(8):
                        row_back(N_EXP // 2, n)

                @block.scalar
                def _(act):
                    n = [0]

                    def link(ins):
                        ins.then_inc(s["chain_act"], 1)
                        n[0] += 1
                        act.wait_ge(s["chain_act"], n[0])

                    def evac(job, ops):
                        act.wait_ge(s["proj_done"], job + 1)
                        for k, (out, src, func, kw) in enumerate(ops):
                            ins = nc.scalar.activation(out, src, func, **kw)
                            if k < len(ops) - 1:
                                link(ins)
                        ins.then_inc(s["proj_free"], 1)

                    def bank(job):
                        return ps[:, BANK_P[job % 2], :]

                    def sum_squares(t):
                        nc.scalar.activation(xn[:, t, :], x[:, t, :], ACT.Square, accum_out=sumsq[:, t:t + 1]).then_inc(s["sumsq_ready"], 1)

                    def root(t, n):
                        act.wait_ge(s["var_ready"], n)
                        nc.scalar.activation(rstd[:, t:t + 1], sumsq[:, t:t + 1], ACT.Sqrt).then_inc(s["sd_ready"], 1)

                    for t in range(NT):
                        sum_squares(t)
                        if t >= 1:
                            root(t - 1, t)
                    root(NT - 1, NT)
                    act.wait_ge(s["small_in"], 16)
                    act.wait_ge(s["bparam_in"], 16)
                    nc.scalar.activation(s5_small[0], small["lstep"], ACT.Exp).then_inc(s["step_ready"], 1)
                    act.wait_ge(s["lam_ready"], 1)
                    nc.scalar.activation(mag, s5_small[2], ACT.Exp).then_inc(s["mag_ready"], 1)
                    act.wait_ge(s["angle_ready"], 1)
                    link(nc.scalar.activation(sin1, sincos[2], ACT.Sin))
                    nc.scalar.activation(cos1, sincos[3], ACT.Sin).then_inc(s["sincos_ready"], 1)
                    for t in range(NT):
                        evac(J_SGU + t, [(z[:, t, :], bank(J_SGU + t), ACT.Gelu_apprx_tanh, {})])
                    act.wait_ge(s["proj_free"], J_SGU + NT)
                    for t in range(NT):
                        ins = nc.scalar.activation(vn[:, t, :], z[:, t, 256:512], ACT.Square, accum_out=vsumsq[:, t:t + 1])
                        if t < NT - 1:
                            link(ins)
                    ins.then_inc(s["vsq_ready"], 1)
                    for c in range(2):
                        evac(J_S5 + c, [(xsT[:, c, :], bank(J_S5 + c), ACT.Identity, {})])
                    act.wait_ge(s["planes_clear"], 2)
                    for c in range(2):
                        b = bank(J_KC + c)
                        evac(J_KC + c, [(c_in[c][0:64, 0, :], b[0:64], ACT.Identity, {}), (c_in[c][64:P, 1, 0:S - 1], b[64:P, 1:S], ACT.Identity, {}),
                                        (c_in[c][64:P, 0, 0:S - 1], b[0:64, 1:S], ACT.Identity, {}), (c_in[c][0:64, 1, :], b[64:P], ACT.Identity, {})])
                        if c == 0:
                            act.wait_ge(s["vvar_ready"], 1)
                            nc.scalar.activation(vrstd, vsumsq, ACT.Sqrt).then_inc(s["vsd_ready"], 1)
                    for i in range(2):
                        evac(J_KS + i, [(q_rot[:, i, :], bank(J_KS + i), ACT.Identity, {})])
                    for i in range(4):
                        evac(J_Q + i, [(q_plain[:, i, :], bank(J_Q + i), ACT.Identity, dict(scale=DH ** -0.5))])
                    for t in range(NT):
                        b = bank(J_V + t)
                        evac(J_V + t, [(v_tok[:, t, :], b[:, 0:256], ACT.Identity, {}),
                                       (nsa_g[:, t, :], b[:, 256:280], ACT.Tanh, dict(scale=0.5))])
                    for c in range(2):
                        act.wait_ge(s["y1_ready"], c + 1)
                        nc.scalar.activation(xsT[:, c, :], xsT[:, c, :], ACT.Gelu_apprx_tanh).then_inc(s["gelu_done"], 1)
                    act.wait_ge(s["hidden_done"], 2)
                    for i in range(2):
                        link(nc.scalar.activation(c_bias[:, i:i + 1], ps[:, BANK_T[i], 62:63], ACT.Identity))
                    act.wait_ge(s["planes_clear"], 5)
                    src = [ps[:, BANK_T[i], 0:62].rearrange("p (a b) -> p a b", a=2) for i in range(2)]
                    nc.scalar.activation(k_hid[:, :, 0:31], src[0], ACT.Gelu_apprx_tanh, bias=c_bias[:, 0:1]).then_inc(s["hid_ready"], 1)
                    nc.scalar.activation(v_hid[:, :, :, 0:31], src[1].unsqueeze(2).to_broadcast([P, G, R, 31]),
                                         ACT.Gelu_apprx_tanh, bias=c_bias[:, 1:2]).then_inc(s["hid_ready"], 1)
                    for m in range(2):
                        act.wait_ge(s["glu_done"], m + 1)
                        nc.scalar.activation(s5T[:, m, :], ps[:, BANK_S[m], :], ACT.Tanh, scale=0.5,
                                             bias=glub_h[:, m:m + 1]).then_inc(s["glu_read"], 1)
                    act.wait_ge(s["h_ready"], NCH)
                    got = [0]

                    def gate(upto):
                        while got[0] < min(upto, 24):
                            j = J_GATE + got[0]
                            evac(j, [(gates[:, got[0], :], bank(j), ACT.Tanh, dict(scale=0.5))])
                            got[0] += 1

                    gate((4 + 8) // ND)
                    act.wait_ge(s["cexp_in"], 1)
                    nc.scalar.activation(c_scf, c_scf, ACT.Exp).then_inc(s["cexp_done"], 1)
                    before = 4 + 8 + 12 + 3
                    gate(before // ND)
                    for i in range(N_ATT):
                        t = (i // 8) % NT
                        nk = (t + 1) * P
                        act.wait_ge(s["max_done"], i + 1)
                        if i >= 2:
                            act.wait_ge(s["tr_done"], i - 1)
                        else:
                            act.wait_ge(s["ct_done"], 2)
                        nc.scalar.activation(prob[i % 2][:, 0:nk], ps[:, BANK_S[i % 2], 0:nk], ACT.Exp, bias=rowmax[:, i % 4:i % 4 + 1],
                                             accum_out=rowsum[:, i:i + 1]).then_inc(s["exp_done"], 1)
                        gate((before + 3 * (i + 1)) // ND)
                    gate(24)
                    for m, (kind, t, half) in enumerate(TAIL):
                        if kind == "mix":
                            act.wait_ge(s["proj_free"], J_TAIL + m + 1)
                            sum_squares(t)
                            root(t, NT + t + 1)
                    act.wait_ge(s["gexp_in"], 1)
                    nc.scalar.activation(gtmp, gtmp, ACT.Exp).then_inc(s["gexp_done"], 1)
                    act.wait_ge(s["e2_in"], 1)
                    nc.scalar.activation(r1[4], r1[4], ACT.Exp).then_inc(s["e2_done"], 1)
                    act.sem_inc(s["silu_done"], CRED)
                    nc.scalar.activation(table_in, ident[:, 0:1], ACT.Identity).then_inc(s["table_in"], 1)
                    act.sem_inc(s["hT_read"], CRED)
                    act.sem_inc(s["y_read"], CRED)
                    act.wait_ge(s["route_done"], 1)
                    with act.Fori(0, N_EXP // 2) as i:
                        for b in range(2):
                            e = 2 * i + b
                            if b == 0:
                                act.wait_ge(s["table_in"], i + 1)
                                nc.scalar.activation(table_in, table_in, ACT.Silu).then_inc(s["table_in"], 1)
                            act.wait_ge(s["gu_done"], e + 1 + CRED)
                            act.wait_ge(s["hid_done"], e + CRED)
                            nc.scalar.activation(silu[0:64], ps[0:64, 0, :], ACT.Silu).then_inc(s["silu_done"], 1)
                            act.wait_ge(s["hT_done"], e + 1 + CRED)
                            act.wait_ge(s["down_done"], e - 1 + CRED)
                            nc.scalar.activation(hidT[b].rearrange("p a b -> p (a b)"), ps[:, 4, 0:256],
                                                 ACT.Identity).then_inc(s["hT_read"], 1)
                            act.wait_ge(s["down_done"], e + 1 + CRED)
                            act.wait_ge(s["selT_read"], i + 1 + CRED)
                            act.wait_ge(s["back_done"], 8 * i + 8)
                            for half in range(2):
                                nc.scalar.activation(y_hi[64 * b:64 * b + 64, half * 512:(half + 1) * 512],
                                                     ps[64 * half:64 * half + 64, 6, :], ACT.Identity,
                                                     scale=w_slot[64 * b:64 * b + 64]).then_inc(s["y_read"], 1)

                @block.vector
                def _(dve):
                    n = [0]
                    v = nc.vector

                    def link(ins):
                        ins.then_inc(s["chain_dve"], 1)
                        n[0] += 1
                        dve.wait_ge(s["chain_dve"], n[0])

                    told = {}

                    def tell(ins, name):
                        ins.then_inc(s[name], 1)
                        told[name] = told.get(name, 0) + 1
                        dve.wait_ge(s[name], told[name])

                    def normalise(k, t):
                        dve.wait_ge(s["sumsq_ready"], NT * k + t + 1)
                        one = slice(t, t + 1)
                        tell(v.tensor_scalar(sumsq[:, one], sumsq[:, one], 1.0 / D, EPS, ALU.mult, ALU.add), "var_ready")
                        dve.wait_ge(s["sd_ready"], NT * k + t + 1)
                        link(v.reciprocal(rstd[:, one], rstd[:, one]))
                        tell(v.tensor_scalar(xn[:, t, :], x[:, t, :], rstd[:, one], None, ALU.mult), "xn_ready")

                    def take_transposed(n, t, half, g):
                        dve.wait_ge(s["proj_done"], n + 1)
                        v.tensor_tensor(hT[:, 4 * half:4 * half + 4, t * P:(t + 1) * P],
                                        ps[:, BANK_P[n % 2], :].rearrange("p (d c) -> p d c", d=4),
                                        g[:, 4 * half:4 * half + 4].unsqueeze(2).to_broadcast([P, 4, P]),
                                        ALU.mult).then_inc(s["proj_free"], 1)

                    _, theta, lam, den, nr, cre, cim, u1, u2, abr, abi = s5_small[:11]

                    def s5_angles():
                        reduce_angle(nc, link, theta, sincos[1], sincos[2], sincos[3])
                        tell(v.tensor_scalar(glub_h, small["glub"], 0.5, None, ALU.mult), "angle_ready")

                    normalise(0, 0)
                    dve.wait_ge(s["small_in"], 16)
                    for t in range(NT):
                        if t + 1 < NT:
                            normalise(0, t + 1)
                        for half in range(2):
                            take_transposed(J_HT + 2 * t + half, t, half, small["gmix"])
                    dve.wait_ge(s["step_ready"], 1)
                    link(v.tensor_tensor(theta, small["a_im"], s5_small[0], ALU.mult))
                    tell(v.tensor_tensor(lam, small["a_re"], s5_small[0], ALU.mult), "lam_ready")
                    s5_angles()
                    dve.wait_ge(s["mag_ready"], 1)
                    dve.wait_ge(s["sincos_ready"], 1)
                    dve.wait_ge(s["bparam_in"], 16)
                    link(v.tensor_tensor(abr, mag, cos1, ALU.mult))
                    link(v.tensor_tensor(abi, mag, sin1, ALU.mult))
                    link(v.tensor_scalar(nr, abr, -1.0, None, ALU.add))
                    link(v.tensor_tensor(u1, small["a_re"], small["a_re"], ALU.mult))
                    link(v.tensor_tensor(u2, small["a_im"], small["a_im"], ALU.mult))
                    link(v.tensor_tensor(den, u1, u2, ALU.add))
                    link(v.reciprocal(den, den))
                    link(v.tensor_tensor(u1, nr, small["a_re"], ALU.mult))
                    link(v.tensor_tensor(u2, abi, small["a_im"], ALU.mult))
                    link(v.tensor_tensor(cre, u1, u2, ALU.add))
                    link(v.tensor_tensor(cre, cre, den, ALU.mult))
                    link(v.tensor_tensor(u1, abi, small["a_re"], ALU.mult))
                    link(v.tensor_tensor(u2, nr, small["a_im"], ALU.mult))
                    link(v.tensor_tensor(cim, u1, u2, ALU.subtract))
                    link(v.tensor_tensor(cim, cim, den, ALU.mult))
                    cre_b = cre.unsqueeze(2).to_broadcast([P, NCH, 32])
                    cim_b = cim.unsqueeze(2).to_broadcast([P, NCH, 32])
                    link(v.tensor_tensor(bbar[:, 0], b_in[:, 0], cre_b, ALU.mult))
                    link(v.tensor_tensor(bb_tmp, b_in[:, 1], cim_b, ALU.mult))
                    link(v.tensor_tensor(bbar[:, 0], bbar[:, 0], bb_tmp, ALU.subtract))
                    link(v.tensor_tensor(bbar[:, 1], b_in[:, 1], cre_b, ALU.mult))
                    link(v.tensor_tensor(bb_tmp, b_in[:, 0], cim_b, ALU.mult))
                    tell(v.tensor_tensor(bbar[:, 1], bbar[:, 1], bb_tmp, ALU.add), "bb_ready")
                    link(v.memset(tab_re[:, :, 0], 1.0))
                    link(v.memset(tab_im[:, :, 0], 0.0))
                    pr, pi, qa, qb = pw
                    link(v.tensor_copy(pr, cos1))
                    link(v.tensor_copy(pi, sin1))
                    m = 1
                    while m < S:
                        t_ = view(tab_tmp, NCH, m)
                        prb = pr.unsqueeze(2).to_broadcast([P, NCH, m])
                        pib = pi.unsqueeze(2).to_broadcast([P, NCH, m])
                        re, im = tab_re[:, :, 0:m], tab_im[:, :, 0:m]
                        re2, im2 = tab_re[:, :, m:2 * m], tab_im[:, :, m:2 * m]
                        link(v.tensor_tensor(re2, re, prb, ALU.mult))
                        link(v.tensor_tensor(t_, im, pib, ALU.mult))
                        link(v.tensor_tensor(re2, re2, t_, ALU.subtract))
                        link(v.tensor_tensor(im2, re, pib, ALU.mult))
                        link(v.tensor_tensor(t_, im, prb, ALU.mult))
                        ins = v.tensor_tensor(im2, im2, t_, ALU.add)
                        m *= 2
                        if m < S:
                            link(ins)
                            link(v.tensor_tensor(qa, pr, pr, ALU.mult))
                            link(v.tensor_tensor(qb, pi, pi, ALU.mult))
                            link(v.tensor_tensor(pi, pi, pr, ALU.mult))
                            link(v.tensor_tensor(pi, pi, pi, ALU.add))
                            link(v.tensor_tensor(pr, qa, qb, ALU.subtract))
                    link(ins)
                    dve.wait_ge(s["bb_done"], 1)
                    tell(v.tensor_copy(view(O_BBT, 512), ps[:, BANK_T[0], :]), "bb_evac")

                    dve.wait_ge(s["vsq_ready"], 1)
                    tell(v.tensor_scalar(vsumsq, vsumsq, 1.0 / 256, EPS, ALU.mult, ALU.add), "vvar_ready")
                    dve.wait_ge(s["vsd_ready"], 1)
                    link(v.reciprocal(vrstd, vrstd))
                    dve.wait_ge(s["sgu_in"], 16)
                    for t in range(NT):
                        tell(v.scalar_tensor_tensor(vn[:, t, :], z[:, t, 256:512], vrstd[:, t:t + 1], sgu_g, ALU.mult, ALU.mult), "vn_ready")
                    for g in range(SG):
                        if g % 2 == 0:
                            dve.wait_ge(s["mixed_done"], g + 2)
                        src = ps[:, BANK_S[g // 2], (g % 2) * 256:(g % 2 + 1) * 256].rearrange("p (a b) -> p a b", a=NT)
                        tell(v.scalar_tensor_tensor(ys[:, :, g * 64:(g + 1) * 64], src, small["sgub"][:, g:g + 1],
                                                    z[:, :, g * 64:(g + 1) * 64], ALU.add, ALU.mult), "mixed_evac")
                    def s5_chunk(j):
                        a, b = s5_ab[j % 2]
                        c, d = s5_c, s5_d
                        cos, sin = tab_re[:, j, :], tab_im[:, j, :]
                        re, im = ps[:, BANK_S[0], :], ps[:, BANK_S[1], :]
                        dve.wait_ge(s["bu_done"], j + 1)
                        if j >= 2:
                            dve.wait_ge(s["y_done"], j - 1)
                        link(v.tensor_tensor(a, re, cos, ALU.mult))
                        link(v.tensor_tensor(c, im, sin, ALU.mult))
                        link(v.tensor_tensor(a, a, c, ALU.add))
                        link(v.tensor_tensor(b, im, cos, ALU.mult))
                        tell(v.tensor_tensor(c, re, sin, ALU.mult), "twist_read")
                        link(v.tensor_tensor(b, b, c, ALU.subtract))
                        m = mag[:, j:j + 1].to_broadcast([P, S])
                        link(v.tensor_tensor_scan(c, m, a, 0.0, ALU.mult, ALU.add))
                        link(v.tensor_tensor_scan(d, m, b, 0.0, ALU.mult, ALU.add))
                        link(v.tensor_tensor(a, c, cos, ALU.mult))
                        link(v.tensor_tensor(b, d, sin, ALU.mult))
                        link(v.tensor_tensor(a, a, b, ALU.subtract))
                        link(v.tensor_tensor(b, d, cos, ALU.mult))
                        link(v.tensor_tensor(c, c, sin, ALU.mult))
                        tell(v.scalar_tensor_tensor(b, b, -1.0, c, ALU.mult, ALU.subtract), "h_ready")

                    def rope(i):
                        dve.wait_ge(s["rot_done"], i + 1)
                        part = ps[:, BANK_T[i % 2], :]
                        c, d = s5_c, s5_d
                        raw = q_rot[:, i, :] if i < 2 else q_plain[:, i - 2, :]
                        link(v.tensor_tensor(c, part, rope_sin, ALU.mult))
                        link(v.tensor_tensor(d, raw, rope_cos, ALU.mult))
                        if i < 2:
                            planes = (k_sel, k_win)[i]
                            dve.wait_ge(s["planes_clear"], 4)
                            link(v.tensor_tensor(planes[0:64, 0, :], c[0:64], d[0:64], ALU.add))
                            tell(v.tensor_tensor(planes[64:P, 1, :], c[64:P], d[64:P], ALU.add), "rope_done")
                        else:
                            tell(v.tensor_tensor(q_rot[:, i - 2, :], c, d, ALU.add), "rope_done")

                    for u in range(NCH):
                        s5_chunk(u)
                        if u == 0:
                            for c in range(2):
                                dve.wait_ge(s["ysT_done"], c + 1)
                                tell(v.tensor_copy(ysT[:, c, :], ps[:, BANK_T[c], :]), "ysT_evac")
                        if 1 <= u <= 6:
                            rope(u - 1)
                    for c in range(2):
                        dve.wait_ge(s["y_done"], 4 * (c + 1))
                        tell(v.scalar_tensor_tensor(xsT[:, c, :], xsT[:, c, :], small["d"][:, c:c + 1], ps[:, BANK_O[c], :],
                                                    ALU.mult, ALU.add), "y1_ready")
                    dve.wait_ge(s["proj_free"], J_V + NT)
                    link(v.tensor_scalar(nsa_g, nsa_g, 1.0, 0.5, ALU.add, ALU.mult))
                    dve.wait_ge(s["hidden_done"], 2)
                    dve.wait_ge(s["planes_clear"], 5)
                    dve.wait_ge(s["ckv_done"], 1)
                    link(v.tensor_copy(k_cmp[0:64, 0, :], ps[0:64, BANK_T[0], 0:32]))
                    link(v.tensor_copy(k_cmp[64:P, 1, :], ps[64:P, BANK_T[0], 32:64]))
                    for r in range(R):
                        ins = v.tensor_copy(v_cmp[32 * r:32 * r + 32, :, r * DH:(r + 1) * DH],
                                            ps[32 * r:32 * r + 32, BANK_T[1], 0:P].rearrange("p (a b) -> p a b", a=2))
                        if r < R - 1:
                            link(ins)
                    tell(ins, "ckv_ready")
                    for m in range(2):
                        dve.wait_ge(s["glu_read"], m + 1)
                        link(v.tensor_scalar(s5T[:, m, :], s5T[:, m, :], 1.0, 0.5, ALU.add, ALU.mult))
                        tell(v.tensor_tensor(s5T[:, m, :], s5T[:, m, :], xsT[:, m, :], ALU.mult), "s5_done")
                    dve.wait_ge(s["cs_done"], 1)
                    dve.wait_ge(s["y_done"], NCH)
                    for b in range(2):
                        src = ps[:, BANK_S[b], :].rearrange("p (t h c) -> p t h c", t=2, h=H)
                        ins = v.tensor_tensor(c_sc[:, 2 * b:2 * b + 2], src,
                                              c_add[:, 2 * b:2 * b + 2, :].unsqueeze(2).to_broadcast([P, 2, H, 32]), ALU.add)
                        if b == 0:
                            link(ins)
                    tell(ins, "cs_read")
                    link(v.tensor_reduce(c_max, c_scf, AX, ALU.max))
                    tell(v.tensor_tensor(c_scf, c_scf, c_max.unsqueeze(2).to_broadcast([P, 32, 32]), ALU.subtract), "cexp_in")
                    dve.wait_ge(s["cexp_done"], 1)
                    link(v.tensor_tensor(c_sc, c_sc, c_01.unsqueeze(2).to_broadcast([P, NT, H, 32]), ALU.mult))
                    link(v.tensor_reduce(c_sum, c_scf, AX, ALU.add))
                    link(v.tensor_scalar(c_sum, c_sum, 1e-30, None, ALU.max))
                    link(v.reciprocal(c_sum, c_sum))
                    link(v.tensor_tensor(c_sum.rearrange("p (t h) -> p t h", t=NT), c_sum.rearrange("p (t h) -> p t h", t=NT),
                                         nsa_g[:, :, 0:24:3], ALU.mult))
                    tell(v.tensor_tensor(c_scf, c_scf, c_sum.unsqueeze(2).to_broadcast([P, 32, 32]), ALU.mult), "cp_ready")
                    for b in range(2):
                        dve.wait_ge(s["ct_done"], b + 1)
                        tell(v.tensor_copy(probT[b], ps[:, BANK_T[b], :]), "ct_evac")
                    dve.wait_ge(s["glu_done"], 2)
                    for t in range(NT):
                        dve.wait_ge(s["oc_done"], t + 1)
                        tell(v.tensor_copy(oacc[:, t, :], ps[:, BANK_O[t % 2], :]), "oc_evac")

                    def out_of(k):
                        br, t = divmod(k, NT)
                        dve.wait_ge(s["pv_done"], 8 * k + 8)
                        link(v.reciprocal(rinv, rowsum[:, 8 * k:8 * k + 8]))
                        link(v.tensor_tensor(wgt, rinv, nsa_g[:, t, 1 + br:24:3], ALU.mult))
                        link(v.tensor_tensor(o_tmp.rearrange("p (h d) -> p h d", h=H),
                                             ps[:, BANK_O[k % 2], :].rearrange("p (h d) -> p h d", h=H),
                                             wgt.unsqueeze(2).to_broadcast([P, H, DH]), ALU.mult))
                        tell(v.tensor_tensor(oacc[:, t, :], oacc[:, t, :], o_tmp, ALU.add), "o_evac")

                    for i in range(N_ATT + 3):
                        if i < N_ATT:
                            nk = ((i // 8) % NT + 1) * P
                            dve.wait_ge(s["scores_done"], i + 1)
                            tell(v.tensor_reduce(rowmax[:, i % 4:i % 4 + 1], ps[:, BANK_S[i % 2], 0:nk], AX, ALU.max, negate=True), "max_done")
                        if 1 <= i <= N_ATT:
                            j = i - 1
                            nk = ((j // 8) % NT + 1) * P
                            dve.wait_ge(s["tr_done"], j + 1)
                            if j >= 2:
                                dve.wait_ge(s["pv_done"], j - 1)
                            tell(v.tensor_copy(probT[j % 2][:, 0:nk], ps[:, BANK_T[j % 2], 0:nk]), "pt_evac")
                        if i >= 3 and (i - 3) % 8 == 7:
                            out_of((i - 3) // 8)
                    for c in range(4):
                        dve.wait_ge(s["oT_done"], c + 1)
                        tell(v.tensor_copy(oT[:, c, :], ps[:, BANK_T[c % 2], :]), "oT_evac")
                    dve.wait_ge(s["proj_free"], J_GATE + 24)
                    m1, m2 = m_tmp
                    for c in range(ND):
                        dve.wait_ge(s["outp_done"], c + 1)
                        link(v.scalar_tensor_tensor(m1, gates[:, c, :], 1.0, ps[:, BANK_S[c % 2], :], ALU.add, ALU.mult))
                        link(v.scalar_tensor_tensor(m2, gates[:, ND + c, :], 1.0, ps[:, BANK_T[c % 2], :], ALU.add, ALU.mult))
                        link(v.tensor_tensor(m1, m1, m2, ALU.add))
                        link(v.scalar_tensor_tensor(m2, gates[:, 2 * ND + c, :], 1.0, ps[:, BANK_O[c % 2], :], ALU.add, ALU.mult))
                        tell(v.tensor_tensor(hT[:, c, :], m1, m2, ALU.add), "merge_done")
                    def add_mix(job, t, half):
                        dve.wait_ge(s["proj_done"], job + 1)
                        xs = x[:, t, half * 512:(half + 1) * 512]
                        v.scalar_tensor_tensor(xs, ps[:, BANK_P[job % 2], :], 0.5, xs, ALU.mult, ALU.add).then_inc(s["proj_free"], 1)

                    for t in range(NT):
                        add_mix(J_MIX + t, t, 0)
                    for m, (kind, t, half) in enumerate(TAIL):
                        if kind == "mix":
                            add_mix(J_TAIL + m, t, half)
                            if t == 0:
                                dve.wait_ge(s["proj_free"], J_TAIL + 1)
                                normalise(1, 0)
                        else:
                            take_transposed(J_TAIL + m, t, half, small["gffn"])
                            if half == 1 and t + 1 < NT:
                                normalise(1, t + 1)

                    link(v.memset(logitT, 0.0))
                    dve.wait_ge(s["rt_done"], 1)
                    dve.wait_ge(s["router_in"], 16)
                    dve.wait_ge(s["mconst_in"], 16)
                    tell(v.tensor_copy(logitT[0:36], ps[0:36, BANK_S[0], :]), "rt_read")
                    dve.wait_ge(s["rt_done"], 2)
                    link(v.tensor_tensor(logit, ps[:, BANK_S[1], 0:144].rearrange("p (a b) -> p a b", a=NT),
                                         rb.unsqueeze(1).to_broadcast([P, NT, 36]), ALU.add))
                    gl = logit[:, :, 0:4]
                    el = logit[:, :, 4:36]

                    def one_hot(out, val, top, desc, w, tmp):
                        link(v.tensor_reduce(top, val, AX, ALU.max))
                        link(v.tensor_tensor(out, val, top.unsqueeze(2).to_broadcast([P, NT, w]), ALU.is_equal))
                        link(v.tensor_tensor(out, out, desc.unsqueeze(1).to_broadcast([P, NT, w]), ALU.mult))
                        link(v.tensor_reduce(tmp, out, AX, ALU.max))
                        link(v.tensor_tensor(out, out, tmp.unsqueeze(2).to_broadcast([P, NT, w]), ALU.is_equal))

                    gmax, gden, top1, top2, e2, first, den1, tmp4, d1, d2 = r1
                    one_hot(goh, gl, gmax, desc4, 4, first)
                    tell(v.tensor_tensor(gtmp, gl, gmax.unsqueeze(2).to_broadcast([P, NT, 4]), ALU.subtract), "gexp_in")
                    link(v.tensor_scalar(goh, goh, 1.0, -NEG, ALU.subtract, ALU.mult))
                    link(v.tensor_tensor(em.rearrange("p t (g e) -> p t g e", g=4), el.rearrange("p t (g e) -> p t g e", g=4),
                                         goh.unsqueeze(3).to_broadcast([P, NT, 4, E_PER]), ALU.add))
                    one_hot(oh[0], em, top1, desc32, 32, first)
                    link(v.scalar_tensor_tensor(em, oh[0], 2 * NEG, em, ALU.mult, ALU.add))
                    one_hot(oh[1], em, top2, desc32, 32, first)
                    tell(v.tensor_tensor(e2, top2, top1, ALU.subtract), "e2_in")
                    tell(v.tensor_tensor(sel_all, oh[0], oh[1], ALU.add), "sel_ready")
                    dve.wait_ge(s["gexp_done"], 1)
                    link(v.tensor_reduce(gden, gtmp, AX, ALU.add))
                    dve.wait_ge(s["e2_done"], 1)
                    link(v.tensor_scalar(den1, e2, 1.0, None, ALU.add))
                    link(v.tensor_tensor(den1, den1, gden, ALU.mult))
                    link(v.reciprocal(cw[0], den1))
                    link(v.tensor_tensor(cw[1], cw[0], e2, ALU.mult))
                    for k in range(2):
                        link(v.tensor_tensor((em, eq)[k], oh[k], cw[k].unsqueeze(2).to_broadcast([P, NT, 32]), ALU.mult))
                    link(v.tensor_tensor(wtab.rearrange("p e t -> p t e"), em, eq, ALU.add))
                    link(v.memset(hid[64:P], 0.0))
                    link(v.memset(slot[:, N_EXP:N_EXP + 2, :], -1.0))
                    link(v.memset(before[:, 0], 0.0))
                    for to in (selT, y_hi[:, 0:512], y_hi[:, 512:D], y_lo[:, 0:512], y_lo[:, 512:D]):
                        v.tensor_scalar(to, ps[:, BANK_P[0], :], 0.0, None, ALU.mult).then_inc(s["pair_zero"], 1)
                    dve.wait_ge(s["rank_done"], 1)
                    tot = ps[:, BANK_T[1], 0:P].rearrange("p (a b) -> p a b", a=NT)
                    link(v.tensor_copy(before[:, 1], tot[:, 0]))
                    for t in range(1, NT):
                        to = before[:, t + 1] if t < NT - 1 else countf[:, 0:N_EXP]
                        link(v.tensor_tensor(to, before[:, t], tot[:, t], ALU.add))
                    link(v.scalar_tensor_tensor(eq, ps[:, BANK_T[0], 0:P].rearrange("p (a b) -> p a b", a=NT), 1.0, before,
                                                ALU.add, ALU.add))
                    link(v.tensor_tensor(eq, eq, sel_all, ALU.mult))
                    link(v.tensor_scalar(slot[:, 0:N_EXP, :].rearrange("p e t -> p t e"), eq, -1.0, None, ALU.add))
                    link(v.tensor_reduce(countf[:, N_EXP:N_EXP + 1], countf[:, 0:N_EXP], AX, ALU.max))
                    tell(v.tensor_copy(counts, countf), "route_done")

                    dve.sem_inc(s["hid_done"], CRED)
                    dve.sem_inc(s["selT_read"], CRED)
                    dve.sem_inc(s["back_added"], 8)
                    dve.sem_inc(s["y_lo_ready"], CRED)

                    def round_rest(i, b):
                        for half in range(2):
                            dve.wait_ge(s["y_read"], 4 * i + 2 * b + half + 1 + CRED)
                            rows, cols = slice(64 * b, 64 * b + 64), slice(half * 512, (half + 1) * 512)
                            v.scalar_tensor_tensor(y_lo[rows, cols], ps[64 * half:64 * half + 64, 6, :], w_slot[rows],
                                                   y_hi[rows, cols], ALU.mult, ALU.subtract).then_inc(s["y_lo_ready"], 1)

                    def add_back(i, n):
                        dve.wait_ge(s["back_done"], 8 * i + n + 1)
                        dve.wait_ge(s["back_added"], 8 * i + n + 1)
                        xs = x[:, n // 2, (n % 2) * 512:(n % 2 + 1) * 512]
                        v.tensor_tensor(xs, xs, ps[:, BANK_BACK[n % 2], :], ALU.add).then_inc(s["back_added"], 1)

                    def take_pair(i, q):
                        dve.wait_ge(s["x_gathered"], i + 1)
                        v.tensor_tensor(xe[q], ps[:, 2:4, :].rearrange("p k (d c) -> p (k d) c", c=2 * CAP), gf(2 * CAP),
                                        ALU.mult).then_inc(s["xe_ready"], 1)

                    build_pair(0).then_inc(s["sel_built"], 1)
                    take_pair(0, 0)
                    with dve.Fori(0, N_EXP // 4) as j:
                        for q in range(2):
                            i = 2 * j + q
                            for b in range(2):
                                e = 2 * i + b
                                if b == 0:
                                    dve.wait_ge(s["selT_done"], i + CRED)
                                    dve.wait_ge(s["sel_built"], i + 1)
                                    v.tensor_tensor(selw.rearrange("p t (b c) -> p t b c", b=2),
                                                    sel.rearrange("p t (b c) -> p t b c", b=2),
                                                    wtab[:, bass.ds(2 * i, 2), :].rearrange("p e t -> p t e").unsqueeze(3)
                                                    .to_broadcast([P, NT, 2, CAP]), ALU.mult).then_inc(s["selw_ready"], 1)
                                    dve.wait_ge(s["selw_ready"], i + 1)
                                    build_pair(i + 1).then_inc(s["sel_built"], 1)
                                    for n in range(6):
                                        add_back(i, n)
                                dve.wait_ge(s["silu_done"], e + 1 + CRED)
                                dve.wait_ge(s["gu_done"], e + 1 + CRED)
                                dve.wait_ge(s["hT_done"], e + CRED)
                                v.tensor_tensor(hid[0:64], ps[64:P, 0, :], silu[0:64], ALU.mult).then_inc(s["hid_done"], 1)
                                if b == 0:
                                    for n in range(6, 8):
                                        add_back(i, n)
                                    dve.wait_ge(s["selT_done"], i + 1 + CRED)
                                    v.tensor_reduce(w_slot, ps[:, 1, :], AX, ALU.max).then_inc(s["slot_weight"], 1)
                                    v.tensor_scalar(selT, ps[:, 1, :], 0.0, None, ALU.is_gt).then_inc(s["slot_weight"], 1)
                                    dve.wait_ge(s["slot_weight"], 2 * i + 2)
                                    dve.sem_inc(s["selT_read"], 1)
                                else:
                                    take_pair(i + 1, 1 - q)
                                round_rest(i, b)
                    for n in range(8):
                        add_back(N_EXP // 2, n)
                    dve.wait_ge(s["back_added"], 8 * (N_EXP // 2) + 16)

                @block.gpsimd
                def _(pool):
                    g = nc.gpsimd
                    n = [0]

                    def link(ins):
                        ins.then_inc(s["chain_pool"], 1)
                        n[0] += 1
                        pool.wait_ge(s["chain_pool"], n[0])

                    cleared = [0]

                    def clear_told(ins):
                        ins.then_inc(s["planes_clear"], 1)
                        cleared[0] += 1
                        pool.wait_ge(s["planes_clear"], cleared[0])

                    pool.wait_ge(s["small_in"], 16)
                    for i in range(2):
                        link(g.memset(c_in[i][:, 2, :], 0.0))
                        clear_told(g.tensor_copy(c_in[i][:, 2, 0:32], small["posk" if i == 0 else "posv"]))
                    for planes in (k_sel, k_win):
                        link(g.memset(planes[64:P, 0, :], 0.0))
                        clear_told(g.memset(planes[0:64, 1, :], 0.0))
                    pool.wait_ge(s["sgu_in"], 16)
                    g.affine_select(out=sgu_w, in_=sgu_w, compare_op=ALU.is_ge, fill=0.0, base=0,
                                    pattern=[[0, SG], [1, P]], channel_multiplier=-1).then_inc(s["sgu_w_ready"], 1)
                    pool.wait_ge(s["sgu_w_ready"], 1)
                    pool.wait_ge(s["hidden_done"], 2)
                    link(g.memset(view(O_CW, 576), 0.0))
                    link(g.memset(k_hid[:, :, 31], 0.0))
                    g.memset(v_hid[:, :, :, 31], 0.0).then_inc(s["planes_clear"], 1)

            most = nc.values_load(counts[0:1, N_EXP:N_EXP + 1], min_val=0, max_val=S)
            with nc.If(most > CAP):
                nc.all_engine_barrier()
                with nc.Fori(1, S // CAP):
                    with nc.Block() as block:
                        @block.vector
                        def _(dve):
                            nc.vector.tensor_scalar(slot, slot, float(CAP), None, ALU.subtract).then_inc(so["ov_shift"], 1)
                            nc.vector.tensor_scalar(countf, countf, float(CAP), None, ALU.subtract).then_inc(so["ov_shift"], 1)
                            dve.wait_ge(so["ov_shift"], 2)
                            nc.vector.tensor_scalar(counts, countf, 0.0, None, ALU.max).then_inc(so["ov_shift"], 1)
                            dve.wait_ge(so["ov_shift"], 3)
                    clear(nc, over_sems)
                    with nc.Fori(0, N_EXP) as e:
                        left = nc.values_load(counts[0:1, bass.ds(e, 1)], min_val=0, max_val=S)
                        with nc.If(left > 0):
                            with nc.Block() as block:
                                @block.sync
                                def _(sp):
                                    for w, name, k in ((w_gate, "expert_w_gate", ND), (w_up, "expert_w_up", ND),
                                                       (w_down, "expert_w_down", NH)):
                                        sp.dma_start(w[0], expert_rows(io[name], e, k)).then_inc(so["ov_weights"], 16)
                                    sp.wait_ge(so["ov_weights"], 48)

                                @block.tensor
                                def _(pe):
                                    pe.wait_ge(so["ov_sel"], 1)
                                    expert_gather(nc, ps, 2, xn, ov_sel[0]).then_inc(so["ov_gathered"], 1)
                                    pe.wait_ge(so["ov_xe"], 1)
                                    pe.wait_ge(so["ov_weights"], 48)
                                    for k in range(ND):
                                        last = expert_gate_up(nc, ps, 0, ov_xe[:, k, :], w_gate[0][:, k, :], w_up[0][:, k, :], k)
                                    last.then_inc(so["ov_gu"], 1)
                                    pe.wait_ge(so["ov_selw"], 1)
                                    for t in range(NT):
                                        last = nc.tensor.transpose(ps[0:CAP, 5, t * P:(t + 1) * P], ov_sel[1][:, t, :], ident)
                                    last.then_inc(so["ov_selT"], 1)
                                    pe.wait_ge(so["ov_hid"], 1)
                                    expert_transpose(nc, ps, hid, ident).then_inc(so["ov_hT"], 1)
                                    pe.wait_ge(so["ov_hT_read"], 1)
                                    for half in range(2):
                                        for k in range(NH):
                                            last = nc.tensor.matmul(ps[0:CAP, 6 + half, :], hidT[0][:, k, :],
                                                                    w_down[0][:, k, half * 512:(half + 1) * 512],
                                                                    start=(k == 0), stop=(k == NH - 1))
                                    last.then_inc(so["ov_down"], 1)
                                    pe.wait_ge(so["ov_selT_read"], 1)
                                    pe.wait_ge(so["ov_y"], 2)
                                    for t in range(NT):
                                        for half in range(2):
                                            nc.tensor.matmul(ps[:, 2 * t + half, :], ov_selT[0:CAP, t * P:(t + 1) * P], ov_y[0:CAP, half * 512:(half + 1) * 512],
                                                             start=True, stop=True).then_inc(so["ov_back"], 1)

                                @block.scalar
                                def _(act):
                                    act.wait_ge(so["ov_gu"], 1)
                                    nc.scalar.activation(silu[0:CAP], ps[0:CAP, 0, :], ACT.Silu).then_inc(so["ov_silu"], 1)
                                    act.wait_ge(so["ov_hT"], 1)
                                    nc.scalar.activation(hidT[0].rearrange("p a b -> p (a b)"), ps[:, 4, 0:256],
                                                         ACT.Identity).then_inc(so["ov_hT_read"], 1)
                                    act.wait_ge(so["ov_selT"], 1)
                                    act.wait_ge(so["ov_hid"], 1)
                                    nc.scalar.activation(ov_selT[0:CAP], ps[0:CAP, 5, :], ACT.Identity).then_inc(so["ov_selT_read"], 1)
                                    act.wait_ge(so["ov_down"], 1)
                                    for half in range(2):
                                        nc.scalar.activation(ov_y[0:CAP, half * 512:(half + 1) * 512], ps[0:CAP, 6 + half, :],
                                                             ACT.Identity).then_inc(so["ov_y"], 1)

                                @block.vector
                                def _(dve):
                                    v = nc.vector
                                    v.tensor_tensor(ov_sel[0], iota.unsqueeze(1).to_broadcast([P, NT, CAP]),
                                                    slot[:, bass.ds(e, 1), :].rearrange("p e t -> p (e t)").unsqueeze(2)
                                                    .to_broadcast([P, NT, CAP]), ALU.is_equal).then_inc(so["ov_sel"], 1)
                                    dve.wait_ge(so["ov_gathered"], 1)
                                    v.tensor_tensor(ov_xe, ps[:, 2, :].rearrange("p (a b) -> p a b", a=ND), gf(CAP), ALU.mult)\
                                     .then_inc(so["ov_xe"], 1)
                                    dve.wait_ge(so["ov_silu"], 1)
                                    v.tensor_tensor(hid[0:CAP], ps[64:P, 0, :], silu[0:CAP], ALU.mult).then_inc(so["ov_hid"], 1)
                                    for n in range(2 * NT):
                                        dve.wait_ge(so["ov_back"], n + 1)
                                        xs = x[:, n // 2, (n % 2) * 512:(n % 2 + 1) * 512]
                                        v.tensor_tensor(xs, xs, ps[:, n, :], ALU.add).then_inc(so["ov_added"], 1)
                                    dve.wait_ge(so["ov_added"], 2 * NT)

                                @block.gpsimd
                                def _(pool):
                                    pool.wait_ge(so["ov_sel"], 1)
                                    nc.gpsimd.tensor_tensor(ov_sel[1], ov_sel[0],
                                                            wtab[:, bass.ds(e, 1), :].rearrange("p e t -> p (e t)").unsqueeze(2)
                                                            .to_broadcast([P, NT, CAP]), ALU.mult).then_inc(so["ov_selw"], 1)
                            clear(nc, over_sems)
                        with nc.Else():
                            nc.sync.sem_clear(so["ov_shift"])
                    nc.all_engine_barrier()

            clear(nc, layer_sems)

        fin = {n: sem(n) for n in ("f_in", "f_sq", "f_var", "f_sd", "f_done", "f_out", "f_chain")}
        gfin = view(O_HT, D)
        with nc.Block() as block:
            @block.sync
            def _(sp):
                sp.dma_start(gfin, io["gfin"].to_broadcast([P, D])).then_inc(fin["f_in"], 16)
                for t in range(NT):
                    sp.wait_ge(fin["f_done"], t + 1)
                    sp.dma_start(io["out"][0, t * P:(t + 1) * P, :], xn[:, t, :]).then_inc(fin["f_out"], 16)
                sp.wait_ge(fin["f_out"], 16 * NT)

            @block.scalar
            def _(act):
                for t in range(NT):
                    nc.scalar.activation(xn[:, t, :], x[:, t, :], ACT.Square, accum_out=sumsq[:, t:t + 1]).then_inc(fin["f_sq"], 1)
                act.wait_ge(fin["f_var"], 1)
                nc.scalar.activation(rstd, sumsq, ACT.Sqrt).then_inc(fin["f_sd"], 1)

            @block.vector
            def _(dve):
                dve.wait_ge(fin["f_sq"], NT)
                nc.vector.tensor_scalar(sumsq, sumsq, 1.0 / D, EPS, ALU.mult, ALU.add).then_inc(fin["f_var"], 1)
                dve.wait_ge(fin["f_sd"], 1)
                nc.vector.reciprocal(rstd, rstd).then_inc(fin["f_chain"], 1)
                dve.wait_ge(fin["f_chain"], 1)
                dve.wait_ge(fin["f_in"], 16)
                for t in range(NT):
                    nc.vector.scalar_tensor_tensor(xn[:, t, :], x[:, t, :], rstd[:, t:t + 1], gfin, ALU.mult, ALU.mult)\
                      .then_inc(fin["f_done"], 1)


N_REDUCE = 8


def reduce_angle(nc, link, ang, kk, rr, r2):
    v = nc.vector
    link(v.tensor_scalar(kk, ang, 1.0 / TWO_PI, MAGIC, ALU.mult, ALU.add))
    link(v.tensor_scalar(kk, kk, MAGIC, None, ALU.subtract))
    link(v.scalar_tensor_tensor(rr, kk, -PI_1, ang, ALU.mult, ALU.add))
    link(v.scalar_tensor_tensor(rr, kk, -PI_2, rr, ALU.mult, ALU.add))
    link(v.scalar_tensor_tensor(rr, kk, -PI_3, rr, ALU.mult, ALU.add))
    link(v.tensor_scalar(rr, rr, PI_SAFE, -PI_SAFE, ALU.min, ALU.max))
    link(v.scalar_tensor_tensor(r2, rr, -1.0, rr, ALU.mult, ALU.max))
    link(v.tensor_scalar(r2, r2, -1.0, float(np.pi / 2), ALU.mult, ALU.add))


def load_expert(nc, sp, io, expert_rows, e, b, w_gate, w_up, w_down, w_sem):
    sp.dma_start(w_gate[b], expert_rows(io["expert_w_gate"], e, ND)).then_inc(w_sem[b][0], 16)
    sp.dma_start(w_up[b], expert_rows(io["expert_w_up"], e, ND)).then_inc(w_sem[b][1], 16)
    sp.dma_start(w_down[b], expert_rows(io["expert_w_down"], e, NH)).then_inc(w_sem[b][2], 16)


def expert_gather(nc, ps, bank, xn, sel):
    for d in range(ND):
        for t in range(NT):
            last = nc.tensor.matmul(ps[:, bank, d * CAP:(d + 1) * CAP], xn[:, t, d * P:(d + 1) * P], sel[:, t, :],
                                    start=(t == 0), stop=(t == NT - 1))
    return last


def expert_gate_up(nc, ps, bank, x_k, wg_k, wu_k, k):
    nc.tensor.matmul(ps[0:64, bank, :], x_k, wg_k, start=(k == 0), stop=(k == ND - 1), tile_position=(0, 0))
    return nc.tensor.matmul(ps[64:P, bank, :], x_k, wu_k, start=(k == 0), stop=(k == ND - 1), tile_position=(0, 64))


def expert_transpose(nc, ps, hid, ident):
    for c in range(NH):
        last = nc.tensor.matmul(ps[:, 4, c * CAP:(c + 1) * CAP], hid[:, c * P:(c + 1) * P], ident[:, 0:CAP], start=True, stop=True)
    return last


def expert_down(nc, ps, bank, hT, wd):
    for k in range(NH):
        for half in range(2):
            last = nc.tensor.matmul(ps[64 * half:64 * half + 64, bank, :], hT[:, k, :], wd[:, k, half * 512:(half + 1) * 512],
                                    start=(k == 0), stop=(k == NH - 1), tile_position=(0, 64 * half))
    return last


def clear(nc, sems):
    nc.all_engine_barrier()
    for x in sems:
        nc.sync.sem_clear(x)
    nc.all_engine_barrier()


def _blocks(a):
    l = a.shape[0]
    return a.reshape((l, 8, 2, 64) + a.shape[3:]).transpose((0, 2, 3, 1) + tuple(range(4, a.ndim + 1))).reshape((l, P, 8) + a.shape[3:])


def _pair_diagonal(a):
    out = np.zeros(a.shape[:3] + (2, 16), a.dtype)
    out[:, 0:64, :, 0] = a[:, 0:64]
    out[:, 64:128, :, 1] = a[:, 64:128]
    return out.reshape(a.shape[:3] + (32,))


def _chunks(a):
    l, r, n = a.shape
    return a.reshape(l, r // P, P, n).transpose(0, 2, 1, 3)


def _flat(*parts):
    return np.ascontiguousarray(np.concatenate([p.reshape(p.shape[0], P, -1) for p in parts], axis=2))


def _constants():
    c = np.zeros((P, N_CONST), np.float32)
    c[:, C_IDENT:C_IDENT + P] = np.eye(P)
    r = np.zeros((P, P), np.float32)
    for h in (0, 64):
        for m in range(HALF_ROPE):
            r[h + m + HALF_ROPE, h + m] = -1.0
            r[h + m, h + m + HALF_ROPE] = 1.0
    c[:, C_ROT:C_ROT + P] = r
    q = np.arange(P)
    c[:, C_CAUSAL:C_CAUSAL + P] = np.where(q[None, :] <= q[:, None], 0.0, NEG)
    t = (np.arange(NT)[None, :, None] * P + q[:, None, None])
    ends = np.arange(32)[None, None, :] * 16 + 31
    ok = (ends <= t) & (np.arange(32)[None, None, :] < NCMP)
    c[:, C_CADD:C_CADD + P] = np.where(ok, 0.0, NEG).reshape(P, P)
    c[:, C_C01:C_C01 + P] = ok.reshape(P, P)
    inv = (np.float32(500000.0) ** (-np.arange(HALF_ROPE, dtype=np.float32) / HALF_ROPE)).astype(np.float32)
    dim = np.arange(P) % DH
    c[:, C_FREQ] = np.where(dim < 2 * HALF_ROPE, inv[dim % HALF_ROPE], 0.0)
    m = np.zeros((P, N_MCONST), np.float32)
    m[:, M_TRI:M_TRI + P] = q[:, None] < q[None, :]
    m[:, M_ONES:M_ONES + P] = 1.0
    m[:, M_IOTA:M_IOTA + CAP] = np.arange(CAP)
    m[:, M_DESC32:M_DESC32 + 32] = 32 - np.arange(32)
    m[:, M_BASE:M_BASE + 32] = np.arange(32) * CAP
    m[:, M_DESC4:M_DESC4 + 4] = 4 - np.arange(4)
    return c, m


def _layout(i):
    a = {k: np.asarray(v) for k, v in i.items()}
    w = _chunks(a["w_in"])
    q = w[..., 0:512].reshape(L, P, ND, G, R, DH).transpose(0, 1, 2, 4, 3, 5).reshape(L, P, ND, 512)
    kc, vc, ks, vs, kw, vw = (w[..., 512 + P * n:512 + P * (n + 1)] for n in range(6))
    nsa, sgu, s5, br = w[..., 1280:1304], w[..., 1304:1816], w[..., 1816:2072], w[..., 2072:5144]

    def two(x):
        return x.reshape(L, 16, 2 * DH, P).transpose(0, 2, 1, 3)
    slabs = [sgu, np.concatenate([s5, kc, vc], 3), np.concatenate([ks, kw, q[..., 0:256]], 3),
             np.concatenate([q[..., 256:512], vs, vw], 3), np.concatenate([two(a["cmp_k_w1"]), two(a["cmp_v_w1"])], 2)]
    slabs += [br[..., n * 512:(n + 1) * 512] for n in range(6)]
    slabs += [_chunks(a["w_attn_o"]), np.concatenate([_chunks(a["w_sgu_o"]), _chunks(a["w_s5_o"])], 2)]
    mix = _chunks(a["w_mix_o"])
    slabs += [mix[..., 0:512], mix[..., 512:1024]]
    dense = np.stack([x.reshape(L, P, SLAB) for x in slabs], axis=1)

    def cols(x, n):
        return x.reshape(L, n, P).transpose(0, 2, 1)

    def pos_rows(x):
        y = np.zeros((L, 2, DH, 32), x.dtype)
        y[:, 0] = x.transpose(0, 2, 1)
        y[:, 1, :, 0:31] = x[:, 1:].transpose(0, 2, 1)
        return y.reshape(L, P, 32)
    pos = [pos_rows(a[k]) for k in ("cmp_pos_k", "cmp_pos_v")]
    w2k = a["cmp_k_w2"]
    step = np.repeat(a["s5_log_step"][:, :, None], 64, axis=2)
    small = _flat(cols(a["norm_mix_g"], 8), cols(a["norm_ffn_g"], 8), _blocks(a["s5_a_re"]), _blocks(a["s5_a_im"]), _blocks(step),
                  cols(a["s5_d"], 2), cols(a["s5_glu_b"], 2), a["sgu_b"].transpose(0, 2, 1), a["cmp_v_w2"],
                  np.concatenate([w2k, w2k], 2), pos[0], pos[1], nsa)
    bparam = _flat(_pair_diagonal(_blocks(a["s5_b_re"])), _pair_diagonal(_blocks(a["s5_b_im"])))
    cc = [_pair_diagonal(_blocks(a[k].transpose(0, 1, 3, 2))) for k in ("s5_c_re", "s5_c_im")]
    cglu = _flat(cc[0], cc[1], _chunks(a["s5_glu_w"]))
    sgup = _flat(a["sgu_w"].transpose(0, 3, 1, 2), np.repeat(a["sgu_norm_g"][:, None, :], P, axis=1))
    rb = np.concatenate([a["router_group_b"], a["router_expert_b"]], 1)
    router = _flat(_chunks(np.concatenate([a["router_group_w"], a["router_expert_w"]], 2)), np.repeat(rb[:, None, :], P, axis=1))
    consts, mconsts = _constants()
    return dict(x=a["x"], positions=a["positions"], dense=dense, small=small, bparam=bparam, cglu=cglu, sgup=sgup, router=router,
                consts=consts, mconsts=mconsts, gfin=a["norm_final_g"][None, :], expert_w_gate=a["expert_w_gate"],
                expert_w_up=a["expert_w_up"], expert_w_down=a["expert_w_down"])


def kernel(**inputs):
    import concourse.bacc as _bacc
    from concourse.bass_utils import run_bass_kernel_spmd as _run

    nc = _bacc.Bacc("TRN2", target_bir_lowering=False, num_devices=1)
    arrays = {f"in_{k}": np.ascontiguousarray(v) for k, v in _layout(inputs).items()}
    io = {k[3:]: nc.dram_tensor(k, v.shape, mybir.dt.from_np(v.dtype), kind="ExternalInput").ap() for k, v in arrays.items()}
    io["out"] = nc.dram_tensor("out_0", (1, S, D), F32, kind="ExternalOutput").ap()
    build(nc, io)
    r = _run(nc, [arrays], core_ids=[0])
    return r.results[0]["out_0"]
```
